# Optimizing a Trainium2 kernel written in Bass

```python
import jax, jax.numpy as jnp
from jax import lax
import numpy as np

D_MODEL = 1024
BATCH = 1
SEQ = 2048
DEPTH = 1
DEC_BATCH = 8
DEC_SEQ = 4
PAST_LEN = 16384
PAGE_SIZE = 128

N_META = 16
D_MIX = D_MODEL
D_POOL = D_MIX // 2
D_REC = D_MIX - D_POOL
POOL_WINDOWS = (2, 4, 8, 16)
N_POOL_GROUPS = len(POOL_WINDOWS)
POOL_GROUP = D_POOL // N_POOL_GROUPS
POOL_BUF = max(POOL_WINDOWS) - 1
REC_HEAD_F = 128
N_REC_HEADS = D_REC // REC_HEAD_F
REC_HEAD_I = D_REC // N_REC_HEADS
REC_CHUNK = 64
D_FF = 2816
CONV_W = 3
D_IN = D_POOL + 4 * D_REC
EPS = 1e-6

kernel_name = 'hymba_pool_hgrn2_convffn_step'

def rmsnorm(x, g):
    xf = x.astype(jnp.float32)
    y = xf * lax.rsqrt(jnp.mean(xf * xf, axis=-1, keepdims=True) + EPS)
    return (y * g.astype(jnp.float32)).astype(x.dtype)

def pool_mix(u, prev, start, w_pool, scale):
    N, T, _ = u.shape
    uf = u.astype(jnp.float32)
    ext = jnp.concatenate([prev.astype(jnp.float32), uf], axis=1)
    c = jnp.concatenate([jnp.zeros((N, 1, D_POOL), jnp.float32), jnp.cumsum(ext, axis=1)], axis=1)
    pos = start + jnp.arange(T)
    P = POOL_BUF
    outs = []
    for gi, w in enumerate(POOL_WINDOWS):
        cs = c[:, :, gi * POOL_GROUP:(gi + 1) * POOL_GROUP]
        win_sum = cs[:, P + 1:P + 1 + T] - cs[:, P + 1 - w:P + 1 - w + T]
        cnt = jnp.minimum(pos + 1, w).astype(jnp.float32)
        outs.append(win_sum / cnt[None, :, None] - uf[:, :, gi * POOL_GROUP:(gi + 1) * POOL_GROUP])
    m = jnp.stack(outs, axis=2)
    y = jnp.einsum('ntgc,gcd->ntgd', m, w_pool.astype(jnp.float32)).reshape(N, T, D_POOL)
    y = y * scale.astype(jnp.float32)
    return y.astype(u.dtype), ext[:, -POOL_BUF:].astype(prev.dtype)

def gla_chunk(S, q, k, g, v):
    C = q.shape[2]
    G = jnp.cumsum(g, axis=2)
    causal = jnp.tril(jnp.ones((C, C), bool))
    diff = G[:, :, :, None, :] - G[:, :, None, :, :]
    decay = jnp.exp(jnp.where(causal[:, :, None], diff, -jnp.inf))
    A = jnp.einsum('nhtd,nhsd,nhtsd->nhts', q, k, decay)
    o = jnp.einsum('nhts,nhsv->nhtv', A, v) + jnp.einsum('nhtd,nhdv->nhtv', q * jnp.exp(G), S)
    G_last = G[:, :, -1:, :]
    S_new = jnp.exp(G_last[:, :, 0, :])[..., None] * S + jnp.einsum('nhsd,nhsv->nhdv', k * jnp.exp(G_last - G), v)
    return o, S_new

def hgrn2_mix(z, S0, lb, g_norm, lead):
    N, T, _ = z.shape
    zf = z.astype(jnp.float32)
    q, f, i, gate = jnp.split(zf, 4, axis=-1)
    q = jax.nn.silu(q) * REC_HEAD_F ** -0.5
    log_f = jnp.logaddexp(jnp.log(lb), jnp.log1p(-lb) + jax.nn.log_sigmoid(f))
    k = (1.0 - lb) * jax.nn.sigmoid(-f)
    heads = lambda a, d: a.reshape(N, T, N_REC_HEADS, d).transpose(0, 2, 1, 3)
    q, k, log_f = heads(q, REC_HEAD_F), heads(k, REC_HEAD_F), heads(log_f, REC_HEAD_F)
    v = heads(i, REC_HEAD_I)
    S = S0.astype(jnp.float32)
    o, S = gla_chunk(S, q[:, :, :lead], k[:, :, :lead], log_f[:, :, :lead], v[:, :, :lead])
    rest = T - lead
    if rest > 0:
        n_c = rest // REC_CHUNK
        blocks = lambda a: a[:, :, lead:].reshape(N, N_REC_HEADS, n_c, REC_CHUNK, a.shape[-1]).transpose(2, 0, 1, 3, 4)

        def step(S, xs):
            o_c, S = gla_chunk(S, *xs)
            return S, o_c

        S, o_rest = lax.scan(step, S, (blocks(q), blocks(k), blocks(log_f), blocks(v)))
        o_rest = o_rest.transpose(1, 2, 0, 3, 4).reshape(N, N_REC_HEADS, rest, REC_HEAD_I)
        o = jnp.concatenate([o, o_rest], axis=2)
    o = o.transpose(0, 2, 1, 3)
    o = o * lax.rsqrt(jnp.mean(o * o, axis=-1, keepdims=True) + EPS) * g_norm.astype(jnp.float32)
    o = o.reshape(N, T, D_REC) * jax.nn.silu(gate)
    return o.astype(z.dtype), S

def conv_ffn(h, prev, w_a, w_b, conv_w, conv_b, w_down):
    T = h.shape[1]
    a = h @ w_a
    b = h @ w_b
    ext = jnp.concatenate([prev.astype(a.dtype), a], axis=1)
    ac = conv_b + sum(conv_w[j] * ext[:, j:j + T] for j in range(CONV_W))
    y = (jax.nn.gelu(ac, approximate=False) * b) @ w_down
    return y, ext[:, -(CONV_W - 1):].astype(prev.dtype)

def trunk_layer(x, pool_prev, pool_start, S0, conv_prev, lead, n1, w_in, w_pool, pool_scale, lb, g_norm,
                w_out, n2, w_a, w_b, conv_w, conv_b, w_down):
    h = rmsnorm(x, n1)
    z = h @ w_in
    y_pool, pool_new = pool_mix(z[..., :D_POOL], pool_prev, pool_start, w_pool, pool_scale)
    y_rec, S_new = hgrn2_mix(z[..., D_POOL:], S0, lb, g_norm, lead)
    x = x + jnp.concatenate([y_pool, y_rec], axis=-1) @ w_out
    y_ffn, conv_new = conv_ffn(rmsnorm(x, n2), conv_prev, w_a, w_b, conv_w, conv_b, w_down)
    return x + y_ffn, pool_new, S_new, conv_new

def setup_inputs(seed: int = 0) -> dict:
    key = jax.random.key(seed)
    ks = jax.random.split(key, 21)
    nrm = lambda k, shape, s: jax.random.normal(k, shape, jnp.float32) * s
    return {
        'x_prompt': nrm(ks[0], (BATCH, SEQ, D_MODEL), 1.0),
        'x_sample': nrm(ks[1], (DEC_BATCH, DEC_SEQ, D_MODEL), 1.0),
        'state_pool': nrm(ks[2], (DEPTH, DEC_BATCH, POOL_BUF, D_POOL), 1.0),
        'state_rec': nrm(ks[3], (DEPTH, DEC_BATCH, N_REC_HEADS, REC_HEAD_F, REC_HEAD_I), 0.3),
        'state_conv': nrm(ks[4], (DEPTH, DEC_BATCH, CONV_W - 1, D_FF), 1.0),
        'meta_tokens': nrm(ks[5], (N_META, D_MODEL), 1.0),
        'norm1_g': 1.0 + nrm(ks[6], (DEPTH, D_MODEL), 0.02),
        'w_in': nrm(ks[7], (DEPTH, D_MODEL, D_IN), D_MODEL ** -0.5),
        'w_pool': nrm(ks[8], (DEPTH, N_POOL_GROUPS, POOL_GROUP, POOL_GROUP), POOL_GROUP ** -0.5),
        'pool_scale': 1.0 + nrm(ks[9], (DEPTH, D_POOL), 0.02),
        'lb_raw': nrm(ks[10], (DEPTH, D_REC), 0.1),
        'rec_norm_g': 1.0 + nrm(ks[11], (DEPTH, REC_HEAD_I), 0.02),
        'w_out': nrm(ks[12], (DEPTH, D_MIX, D_MODEL), D_MIX ** -0.5),
        'norm2_g': 1.0 + nrm(ks[13], (DEPTH, D_MODEL), 0.02),
        'w_a': nrm(ks[14], (DEPTH, D_MODEL, D_FF), D_MODEL ** -0.5),
        'w_b': nrm(ks[15], (DEPTH, D_MODEL, D_FF), D_MODEL ** -0.5),
        'conv_w': nrm(ks[16], (DEPTH, CONV_W, D_FF), CONV_W ** -0.5),
        'conv_b': nrm(ks[17], (DEPTH, D_FF), 0.01),
        'w_down': nrm(ks[18], (DEPTH, D_FF, D_MODEL), D_FF ** -0.5),
        'final_g': 1.0 + nrm(ks[19], (D_MODEL,), 0.02),
    }

def reference(x_prompt, x_sample, state_pool, state_rec, state_conv, meta_tokens, norm1_g, w_in, w_pool,
              pool_scale, lb_raw, rec_norm_g, w_out, norm2_g, w_a, w_b, conv_w, conv_b, w_down, final_g):
    lb_all = jnp.cumsum(jax.nn.softmax(lb_raw.astype(jnp.float32), axis=0), axis=0)
    lb_all = lb_all - lb_all[:1]
    B = x_prompt.shape[0]
    xp = jnp.concatenate([jnp.broadcast_to(meta_tokens[None].astype(x_prompt.dtype), (B, N_META, D_MODEL)), x_prompt], axis=1)
    xs = x_sample
    pool_p0 = jnp.zeros((B, POOL_BUF, D_POOL), state_pool.dtype)
    rec_p0 = jnp.zeros((B, N_REC_HEADS, REC_HEAD_F, REC_HEAD_I), jnp.float32)
    conv_p0 = jnp.zeros((B, CONV_W - 1, D_FF), state_conv.dtype)
    pool_p, rec_p, conv_p, pool_s, rec_s, conv_s = [], [], [], [], [], []
    for l in range(DEPTH):
        lp = (norm1_g[l], w_in[l], w_pool[l], pool_scale[l], lb_all[l], rec_norm_g[l], w_out[l], norm2_g[l],
              w_a[l], w_b[l], conv_w[l], conv_b[l], w_down[l])
        xp, pp, sp, cp = trunk_layer(xp, pool_p0, 0, rec_p0, conv_p0, N_META, *lp)
        xs, ps, ss, cs = trunk_layer(xs, state_pool[l], PAST_LEN, state_rec[l], state_conv[l], xs.shape[1], *lp)
        pool_p.append(pp); rec_p.append(sp.astype(state_rec.dtype)); conv_p.append(cp)
        pool_s.append(ps); rec_s.append(ss.astype(state_rec.dtype)); conv_s.append(cs)
    y_prompt = rmsnorm(xp, final_g)[:, N_META:]
    y_sample = rmsnorm(xs, final_g)
    return (y_prompt, y_sample, jnp.stack(pool_p), jnp.stack(rec_p), jnp.stack(conv_p),
            jnp.stack(pool_s), jnp.stack(rec_s), jnp.stack(conv_s))


_drawn_inputs = setup_inputs


def setup_inputs(seed=0):
    import zlib

    import numpy as np

    out = dict(_drawn_inputs(seed))
    spreads = {}
    factors = {'meta_tokens': 4.452,
     'pool_scale': 5.268,
     'rec_norm_g': 6.982,
     'norm2_g': 2.751,
     'conv_b': 8.0,
     'final_g': 2.843}
    for name, (base, spread) in spreads.items():
        noise = np.random.default_rng([zlib.crc32(name.encode()), seed]).standard_normal(out[name].shape)
        drawn = base * np.exp(spread * noise) if base else spread * noise
        out[name] = __import__('jax').numpy.asarray(drawn.astype(out[name].dtype))
    for name, factor in factors.items():
        out[name] = (out[name] * factor).astype(out[name].dtype)
    return out
```

```python
from contextlib import ExitStack, contextmanager

import numpy as np

import concourse.bass as bass
from concourse import mybir

F32 = mybir.dt.float32
F32R = mybir.dt.float32r
ALU = mybir.AluOpType
ACT = mybir.ActivationFunctionType

P = 128
D_MODEL = 1024
SEQ = 2048
DEC_BATCH = 8
DEC_SEQ = 4
N_META = 16
D_POOL = 512
POOL_BUF = 15
HEADS = 4
D_FF = 2816
EPS = 1e-6
Q_SCALE = float(P) ** -0.5
WINDOWS = (2, 4, 8, 16)

SAMPLES = DEC_BATCH * DEC_SEQ
HEAD = N_META + SAMPLES
SEQS = 1 + DEC_BATCH
BLOCK = 512
BLOCKS = SEQ // BLOCK
TILES = BLOCK // P
WIDE = HEAD + BLOCK
KD = D_MODEL // P
FT = D_FF // P
UNIT = 1024
UNITS = 96
U_F, U_Q, U_GATE, U_V, U_U, U_OUT, U_UP, U_DOWN = 0, 4, 8, 12, 16, 20, 28, 72
LEVELS = 7
HEAD_LEVELS = 4
EXT = POOL_BUF + N_META
NEXT_AT = 3
AHEAD = {TILES * (h - 1) - 1 + n: (h, (2 * n, 2 * n + 1)) for h in (2, 3) for n in range(4)}

C_IDENT = 0
C_MASK = C_IDENT + P
C_RESET = C_MASK + (1 + LEVELS) * P
C_HMASK = C_RESET + WIDE
C_SEQ = C_HMASK + (1 + HEAD_LEVELS) * HEAD
C_COUNT = C_SEQ + SEQS
C_END = C_COUNT + len(WINDOWS) * N_META

V_CONV_W, V_CONV_B, V_N1, V_N2, V_LB, V_SCALE, V_END = 0, 66, 88, 96, 104, 108, 112


def shape_tables():
    t = np.zeros((P, C_END), np.float32)
    t[:, C_IDENT:C_IDENT + P] = np.eye(P)
    s, q = np.arange(P)[:, None], np.arange(P)[None, :]

    def level(h):
        return (s // (2 * h) == q // (2 * h)) & (s % (2 * h) < h) & (q % (2 * h) >= h)

    t[:, C_MASK:C_MASK + P] = np.eye(P) * Q_SCALE
    for n in range(LEVELS):
        t[:, C_MASK + (n + 1) * P:C_MASK + (n + 2) * P] = level(2 ** n) * Q_SCALE
    reset = np.ones(WIDE, np.float32)
    reset[0] = 0
    reset[N_META:HEAD:DEC_SEQ] = 0
    reset[HEAD::P] = 0
    t[:, C_RESET:C_RESET + WIDE] = reset
    t[:HEAD, C_HMASK:C_HMASK + HEAD] = np.eye(HEAD) * Q_SCALE
    for n in range(HEAD_LEVELS):
        m = level(2 ** n)[:HEAD, :HEAD] * Q_SCALE
        if 2 ** n >= DEC_SEQ:
            m[:, N_META:] = 0
        t[:HEAD, C_HMASK + (n + 1) * HEAD:C_HMASK + (n + 2) * HEAD] = m
    t[:N_META, C_SEQ] = 1
    for n in range(DEC_BATCH):
        t[N_META + n * DEC_SEQ:N_META + (n + 1) * DEC_SEQ, C_SEQ + 1 + n] = 1
    for g, w in enumerate(WINDOWS):
        t[:, C_COUNT + g * N_META:C_COUNT + (g + 1) * N_META] = 1.0 / np.minimum(np.arange(N_META) + 1, w)
    return t


class Order:

    def __init__(self, engine, sem):
        self.engine, self.sem, self.base, self.n = engine, sem, 0, 0

    def mark(self, instruction):
        instruction.then_inc(self.sem, 1)
        self.n += 1

    def settle(self):
        self.engine.wait_ge(self.sem, self.base + self.n)

    @contextmanager
    def loop(self, lo, hi, marks):
        base, n = self.base, self.n
        with self.engine.Fori(lo, hi) as i:
            self.base, self.n = base + n + (i - lo) * marks, 0
            yield i
            assert self.n == marks, (self.n, marks)
        self.base, self.n = base, n + (hi - lo) * marks


def trunk_step(nc, x_prompt, x_sample, state_pool, state_rec, state_conv, meta_tokens, vectors, w_in, w_pool,
               rec_norm_g, w_out, w_a, w_b, w_down, final_g, tables,
               y_prompt, y_sample, pool_prompt, rec_prompt, conv_prompt, pool_sample, rec_sample, conv_sample):
    with ExitStack() as ctx:
        def sb(name, shape, dt=F32):
            return ctx.enter_context(nc.sbuf_tensor(name, shape, dt))

        def sem(name):
            return ctx.enter_context(nc.semaphore(name))

        h_hi = sb("h_hi", [P, KD, WIDE], F32R)
        h_lo = sb("h_lo", [P, KD, WIDE], F32R)
        x_tok = sb("x_tok", [P, TILES + 1, D_MODEL])
        with nc.sbuf_tensor("w_raw", [P, 4, UNIT], F32) as w_raw:
            pass
        w_lo = sb("w_lo", [P, 4, UNIT], F32R)
        w_hi = sb("w_hi", [P, 4, UNIT], F32R)
        with nc.sbuf_tensor("pooled", [P, HEADS, WIDE], F32) as pooled:
            pass
        act_hi = sb("act_hi", [P, 2, WIDE], F32R)
        act_lo = sb("act_lo", [P, 2, WIDE], F32R)
        tab = sb("tab", [P, C_END])
        vec = sb("vec", [P, V_END])
        wp = sb("wp", [P, HEADS, P])
        fg = sb("fg", [P, D_MODEL])
        gn = sb("gn", [P, P])
        state = sb("state", [P, HEADS, P])
        conv_hist = sb("conv_hist", [P, FT, 2])
        u_hist = sb("u_hist", [P, HEADS, POOL_BUF])
        sumsq = sb("sumsq", [P, TILES + 1])
        var = sb("var", [P, TILES + 1])
        rstd = sb("rstd", [P, TILES + 1])
        rtmp = sb("rtmp", [P, TILES + 1])
        osumsq = sb("osumsq", [P, TILES + 1, HEADS])
        ovar = sb("ovar", [P, (TILES + 1) * HEADS])
        orstd = sb("orstd", [P, (TILES + 1) * HEADS])
        ortmp = sb("ortmp", [P, (TILES + 1) * HEADS])
        lb = sb("lb", [P, 4, HEADS])
        o_junk = sb("o_junk", [P, P])
        g_end = sb("g_end", [P, HEADS, TILES])
        arena = sb("arena", [P, 23776])
        ps = ctx.enter_context(nc.psum_tensor("ps", [P, 8, 512], F32))

        ident = tab[:, C_IDENT:C_IDENT + P]
        masks = tab[:, C_MASK:C_MASK + (1 + LEVELS) * P]
        reset = tab[:, C_RESET:C_RESET + WIDE]
        hmasks = tab[0:HEAD, C_HMASK:C_HMASK + (1 + HEAD_LEVELS) * HEAD]
        gain = [vec[:, V_N1:V_N1 + KD], vec[:, V_N2:V_N2 + KD]]

        def part(at, *shape):
            n = int(np.prod(shape))
            v = arena[:, at:at + n]
            if len(shape) == 2:
                return v.rearrange("p (a b) -> p a b", a=shape[0])
            if len(shape) == 3:
                return v.rearrange("p (a b c) -> p a b c", a=shape[0], b=shape[1])
            return v

        xn = part(12320, 2, D_MODEL)
        t32 = part(14368, 2, 512)
        junk = part(22752, D_MODEL)
        x_next = part(15392, TILES, D_MODEL)
        q_t = part(0, HEADS, WIDE)
        k_t = part(2240, HEADS, WIDE)
        g_t = part(4480, HEADS, WIDE)
        gate = part(6720, TILES + 1, 512)
        v_tok = part(9280, TILES + 1, 512)
        f_u = part(11840, 2, WIDE)
        f_low = part(12960, 2, WIDE)
        f_r = part(14080, WIDE)
        m_lv = [part(11840, LEVELS, BLOCK), part(15424, LEVELS, BLOCK)]
        dec = part(19008, 2, BLOCK)
        u_sum = part(19008, 2, POOL_BUF + BLOCK)
        u_ext = part(20062, 2, POOL_BUF + BLOCK)
        a_all = part(20062, (1 + LEVELS) * P)
        a_t = part(21116, 2, P)
        kd_tok = part(21372, 2, P)
        kd = part(21628, 2, BLOCK)
        qe = part(22652, 2, BLOCK)
        hu_ext = part(15424, SEQS, EXT)
        hu_sum = part(15703, 2, SEQS * EXT)
        pool_rows = part(16261, 512)
        u_rows = part(16773, HEADS * SAMPLES)
        pool_in = part(16901, HEADS * DEC_BATCH * POOL_BUF)
        s0 = part(15424, DEC_BATCH, P)
        v_seq = part(16448, SEQS, P)
        h_lv = part(17600, HEAD_LEVELS, HEAD)
        h_dec = part(17792, 2 + HEAD_LEVELS, HEAD)
        ha_all = part(18080, (1 + HEAD_LEVELS) * HEAD)
        ha_t = part(18320, HEAD)
        o_feat = part(18368, HEAD)
        h_kd = part(18416, HEAD)
        h_qe = part(18464, HEAD)
        acts = part(0, FT, WIDE)
        a_ext = part(12320, 2, 2 + BLOCK)
        conv = part(13348, 2, BLOCK)
        gelu = part(14372, 2, BLOCK)
        ha_ext = part(15396, 2, SEQS * (2 + N_META))
        hconv = part(15720, 2, SEQS * N_META)
        conv_rows = part(16008, D_FF)
        conv_in = part(18824, FT, 2 * DEC_BATCH)
        conv_out = part(19176, FT, 2 * DEC_BATCH)
        last_rows = part(0, D_POOL)

        raw_loaded = [sem(f"raw_loaded{s}") for s in range(4)]
        w_slot_free = sem("w_slot_free")
        w_hi_ready, w_ready, unit_done = sem("w_hi_ready"), sem("w_ready"), sem("unit_done")
        tab_loaded, vec_loaded, small_loaded = sem("tab_loaded"), sem("vec_loaded"), sem("small_loaded")
        pool_state_loaded, conv_state_loaded, rec_state_loaded = (
            sem("pool_state_loaded"), sem("conv_state_loaded"), sem("rec_state_loaded"))
        x_loaded = [sem(f"x_loaded{t}") for t in range(TILES)]
        x_next_loaded = [sem(f"x_next_loaded{t}") for t in range(TILES)]
        hx_loaded = sem("hx_loaded")
        dve_order, act_order = sem("dve_order"), sem("act_order")
        setup_t, vec_ready, lb_exp, setup_done = sem("setup_t"), sem("vec_ready"), sem("lb_exp"), sem("setup_done")
        squared, hsquared, var_ready, guess_ready = sem("squared"), sem("hsquared"), sem("var_ready"), sem("guess_ready")
        xn_ready, hxn_ready, xt_done, hxt_done = sem("xn_ready"), sem("hxn_ready"), sem("xt_done"), sem("hxt_done")
        t32_ready, ht32_ready, h_hi_ready, hh_hi_ready = (
            sem("t32_ready"), sem("ht32_ready"), sem("h_hi_ready"), sem("hh_hi_ready"))
        h_ready, hh_ready = sem("h_ready"), sem("hh_ready")
        f_taken, f_exp, f_sig, f_ln, g_ready = sem("f_taken"), sem("f_exp"), sem("f_sig"), sem("f_ln"), sem("g_ready")
        q_taken, u_taken, gate_taken, v_taken = sem("q_taken"), sem("u_taken"), sem("gate_taken"), sem("v_taken")
        pooled_ready, pool_done, pool_hi, pool_taken = (
            sem("pooled_ready"), sem("pool_done"), sem("pool_hi"), sem("pool_taken"))
        pool_in_t, pool_in_taken, u_rows_t, u_rows_ready = (
            sem("pool_in_t"), sem("pool_in_taken"), sem("u_rows_t"), sem("u_rows_ready"))
        dec_ready, dec_exp, kd_ready, eg_ready, qe_ready, lv_ready = (
            sem("dec_ready"), sem("dec_exp"), sem("kd_ready"), sem("eg_ready"), sem("qe_ready"), sem("lv_ready"))
        a_done, a_masked, at_ready, kdt_done, kdt_ready, o_done, su_done, s_ready = (
            sem("a_done"), sem("a_masked"), sem("at_ready"), sem("kdt_done"), sem("kdt_ready"),
            sem("o_done"), sem("su_done"), sem("s_ready"))
        o_squared, o_gated = sem("o_squared"), sem("o_gated")
        hdec_ready, hdec_exp, hops_ready, ha_done, hat_ready = (
            sem("hdec_ready"), sem("hdec_exp"), sem("hops_ready"), sem("ha_done"), sem("hat_ready"))
        hkdt_done, hkdt_ready, hof_done, hof_ready, ho_done, ho_squared, ho_gated = (
            sem("hkdt_done"), sem("hkdt_ready"), sem("hof_done"), sem("hof_ready"), sem("ho_done"),
            sem("ho_squared"), sem("ho_gated"))
        v_seq_ready, hs_done, hs_ready, rec_stored = (
            sem("v_seq_ready"), sem("hs_done"), sem("hs_ready"), sem("rec_stored"))
        ovar_ready, oguess_ready, y_ready, yt_done, y_hi, y_taken = (
            sem("ovar_ready"), sem("oguess_ready"), sem("y_ready"), sem("yt_done"), sem("y_hi"), sem("y_taken"))
        x1_ready, hx1_ready = sem("x1_ready"), sem("hx1_ready")
        a_taken, conv_ready, gelu_ready, act_ready = (
            sem("a_taken"), sem("conv_ready"), sem("gelu_ready"), sem("act_ready"))
        hist_ready, ha_taken, hconv_ready, hgelu_ready, hb_taken = (
            sem("hist_ready"), sem("ha_taken"), sem("hconv_ready"), sem("hgelu_ready"), sem("hb_taken"))
        conv_in_t, conv_in_ready, conv_out_t, conv_out_taken = (
            sem("conv_in_t"), sem("conv_in_ready"), sem("conv_out_t"), sem("conv_out_taken"))
        act_hi_ready, act_lo_ready, act0_used = sem("act_hi_ready"), sem("act_lo_ready"), sem("act0_used")
        x2_ready, hx2_ready, out_ready, hout_ready = (
            sem("x2_ready"), sem("hx2_ready"), sem("out_ready"), sem("hout_ready"))
        y_stored = [sem(f"y_stored{t}") for t in range(TILES)]
        stored, last_t, last_taken = sem("stored"), sem("last_t"), sem("last_taken")

        block = ctx.enter_context(nc.Block())

        def win(w):
            return slice(w * P, (w + 1) * P)

        def main(t):
            return slice(HEAD + P * t, HEAD + P * (t + 1))

        def bank(half, tile):
            return (half * (TILES + 1) + tile) % 8

        @block.sync
        def _(sp):
            def unit(b, slot, u, dst, src):
                if not (isinstance(b, int) and isinstance(u, int) and b == 0 and u < 4):
                    sp.wait_ge(unit_done, b * UNITS + u - 3)
                sp.dma_start(dst, src).then_inc(raw_loaded[slot], 16)

            def raw(slot, k):
                return w_raw[:, slot, :].rearrange("p (k n) -> p k n", k=k)

            w_in_t = w_in.rearrange("(k p) n -> p k n", p=P)
            wout = w_out.rearrange("(k p) n -> p k n", p=P)
            wa = w_a.rearrange("(k p) n -> p k n", p=P)
            wb = w_b.rearrange("(k p) n -> p k n", p=P)
            wdown = w_down.rearrange("(k p) n -> p k n", p=P)

            def body(b):
                for s in range(4):
                    unit(b, s, U_F + s, raw(s, KD), w_in_t[:, :, 1024 + s * P:1024 + (s + 1) * P])
                for s in range(4):
                    unit(b, s, U_Q + s, raw(s, KD), w_in_t[:, :, 512 + s * P:512 + (s + 1) * P])
                if not isinstance(b, int):
                    store_y(b - 1)
                for s in range(4):
                    unit(b, s, U_GATE + s, raw(s, 2), w_in_t[:, 2 * s:2 * s + 2, 2048:2560])
                if not isinstance(b, int):
                    for t in range(TILES):
                        sp.wait_ge(y_stored[t], 16 * b)
                        sp.dma_start(x_tok[:, t, :], x_prompt[bass.ds(b * BLOCK + P * t, P), :]).then_inc(
                            x_loaded[t], 16)
                for s in range(4):
                    unit(b, s, U_V + s, raw(s, 2), w_in_t[:, 2 * s:2 * s + 2, 1536:2048])
                for s in range(4):
                    unit(b, s, U_U + s, raw(s, KD), w_in_t[:, :, s * P:(s + 1) * P])
                for n in range(2):
                    for s in range(4):
                        unit(b, s, U_OUT + 4 * n + s, raw(s, 2), wout[:, 2 * s:2 * s + 2, n * 512:(n + 1) * 512])
                with sp.Fori(0, FT // 2) as j:
                    for s in range(4):
                        src = (wa, wb)[s % 2]
                        unit(b, s, U_UP + 4 * j + s, raw(s, KD), src[:, :, bass.ds((2 * j + s // 2) * P, P)])
                for n in range(2):
                    cols = slice(n * 512, (n + 1) * 512)
                    for j in range(2):
                        for s in range(4):
                            unit(b, s, U_DOWN + 12 * n + 4 * j + s, raw(s, 2),
                                 wdown[:, 8 * j + 2 * s:8 * j + 2 * s + 2, cols])
                        if (n, j) == (0, 0):
                            sp.wait_ge(act_hi_ready, 2 * FT * b + 1)
                            for t in range(TILES):
                                sp.dma_start(x_next[:, t, :],
                                             x_prompt[bass.ds((b + 1) % BLOCKS * BLOCK + P * t, P), :]).then_inc(
                                                 x_next_loaded[t], 16)
                    for s in range(4):
                        k = (16, 18, 20, 20)[s]
                        unit(b, s, U_DOWN + 12 * n + 8 + s, raw(s, 2), wdown[:, k:k + 2, cols])

            def store_y(b):
                for t in range(TILES):
                    sp.wait_ge(out_ready, 4 * b + t + 1)
                    sp.dma_start(y_prompt[bass.ds(b * BLOCK + P * t, P), :], x_tok[:, t, :]).then_inc(y_stored[t], 16)

            sp.dma_start(tab[:, :], tables).then_inc(tab_loaded, 16)
            sp.dma_start(junk[0:V_END, 0:P], vectors).then_inc(vec_loaded, 16)
            for t in range(TILES):
                sp.dma_start(x_tok[:, t, :], x_prompt[P * t:P * (t + 1), :]).then_inc(x_loaded[t], 16)
            sp.dma_start(x_tok[0:N_META, TILES, :], meta_tokens).then_inc(hx_loaded, 16)
            sp.dma_start(x_tok[N_META:HEAD, TILES, :], x_sample).then_inc(hx_loaded, 16)
            sp.dma_start(pool_rows[0:DEC_BATCH * POOL_BUF, :], state_pool.rearrange("n t c -> (n t) c")).then_inc(
                pool_state_loaded, 16)
            sp.dma_start(wp[:, :, :], w_pool.rearrange("g c d -> c g d")).then_inc(small_loaded, 16)
            sp.dma_start(fg[:, :], final_g.rearrange("(a d) -> a d", a=1).broadcast_to([P, D_MODEL])).then_inc(
                small_loaded, 16)
            sp.dma_start(gn[:, :], rec_norm_g.broadcast_to([P, P])).then_inc(small_loaded, 16)
            sp.dma_start(pool_sample[:, 0:POOL_BUF - DEC_SEQ, :], state_pool[:, DEC_SEQ:POOL_BUF, :]).then_inc(stored, 16)
            body(0)
            with sp.Fori(1, BLOCKS) as b:
                body(b)
            store_y(BLOCKS - 1)
            for h in range(HEADS):
                sp.wait_ge(s_ready, BLOCKS * HEADS * TILES)
                sp.dma_start(rec_prompt[h], state[:, h, :]).then_inc(stored, 16)
            sp.wait_ge(last_taken, 1)
            sp.dma_start(pool_prompt, last_rows[0:POOL_BUF, :]).then_inc(stored, 16)
            sp.wait_ge(last_taken, 2)
            sp.dma_start(conv_prompt, conv_rows[0:2, :]).then_inc(stored, 16)
            for t in range(TILES):
                sp.wait_ge(y_stored[t], 16 * BLOCKS)
            sp.wait_ge(stored, 16 * (1 + HEADS + 2))

        @block.gpsimd
        def _(pool):
            def units(j):
                for s in range(4):
                    pool.wait_ge(raw_loaded[s], 16 * (j + 1))
                    pool.sem_inc(w_slot_free, 1)
                    nc.gpsimd.tensor_scalar(w_hi[:, s, :], w_raw[:, s, :], 1.0, 1.0, ALU.mult, ALU.mult).then_inc(
                        w_hi_ready, 1)
                    pool.wait_ge(w_hi_ready, 4 * j + s + 1)
                    nc.gpsimd.tensor_tensor(w_lo[:, s, :], w_raw[:, s, :], w_hi[:, s, :].bitcast(F32),
                                            ALU.subtract).then_inc(w_ready, 1)

            with pool.Fori(0, BLOCKS * UNITS // 4) as j:
                units(j)

        @block.tensor
        def _(pe):
            def three(out, lhs, rhs, first, last):
                nc.tensor.matmul(out, lhs[0], rhs[0], start=first, stop=False)
                nc.tensor.matmul(out, lhs[1], rhs[0], start=False, stop=False)
                return nc.tensor.matmul(out, lhs[0], rhs[1], start=False, stop=last)

            def wslot(s, k):
                return [w[:, s, :].rearrange("p (k n) -> p k n", k=k) for w in (w_hi, w_lo)]

            def features(s, out, cols):
                w = wslot(s, KD)
                for k in range(KD):
                    last = three(out, (w[0][:, k, :], w[1][:, k, :]), (h_hi[:, k, cols], h_lo[:, k, cols]),
                                 k == 0, k == KD - 1)
                return last

            MAIN = slice(HEAD, WIDE)

            def row_transposes(n, t, first_bank, bank_free):
                pe.wait_ge(xn_ready, n + t + 1)
                for half in range(2):
                    if t >= bank_free:
                        pe.wait_ge(t32_ready, 2 * (n + t - bank_free) + half + 1)
                    for k in range(4):
                        last = nc.tensor.transpose(
                            ps[:, first_bank + half, k * P:(k + 1) * P],
                            xn[:, t % 2, (4 * half + k) * P:(4 * half + k + 1) * P], ident)
                    last.then_inc(xt_done, 1)

            def norm_transposes(b, w, hd):
                n = 8 * b + 4 * w
                for t in range(TILES):
                    row_transposes(n, t, 2 * (t % 2), 2)
                if hd:
                    pe.wait_ge(hxn_ready, w + 1)
                    for k in range(KD):
                        last = nc.tensor.transpose(ps[:, 4, k * HEAD:(k + 1) * HEAD], xn[0:HEAD, 0, k * P:(k + 1) * P],
                                                   ident[0:HEAD, 0:HEAD])
                    last.then_inc(hxt_done, 1)
                pe.wait_ge(h_ready, 2 * (n + TILES))
                if hd:
                    pe.wait_ge(hh_ready, 2 * w + 1)

            def feature_tile(b, u, i, bank_main, bank_head, hd):
                pe.wait_ge(w_ready, UNITS * b + u + 1)
                last = features(u % 4, ps[:, bank_main, :], MAIN)
                if hd:
                    last = features(u % 4, ps[:, bank_head, 0:HEAD], slice(0, HEAD))
                last.then_inc(unit_done, 1)

            def token_tiles(b, u0, banks, hbank, hd):
                for i in range(4):
                    pe.wait_ge(w_ready, UNITS * b + u0 + i + 1)
                    w = wslot((u0 + i) % 4, 2)
                    for kk in range(2):
                        k = 2 * i + kk
                        first, fin = k == 0, k == KD - 1
                        for t in range(TILES + hd):
                            cols = main(t) if t < TILES else slice(0, HEAD)
                            out = ps[:, banks[t], :] if t < TILES else ps[0:HEAD, hbank, :]
                            last = three(out, (h_hi[:, k, cols], h_lo[:, k, cols]),
                                         (w[0][:, kk, :], w[1][:, kk, :]), first, fin)
                    last.then_inc(unit_done, 1)

            def attention(b):
                def scores(i):
                    h, w, n = i // TILES, i % TILES, 16 * b + i
                    if i == 0:
                        pe.wait_ge(g_ready, 4 * b + HEADS)
                    if w == 0:
                        pe.wait_ge(lv_ready, LEVELS * (4 * b + h + 1))
                    if not (isinstance(n, int) and n < 2):
                        pe.wait_ge(a_masked, n - 1)
                    c = main(w)
                    for l in range(1 + LEVELS):
                        out = ps[:, 2 * (i % 2) + l // 4, win(l % 4)]
                        if l == 0:
                            last = nc.tensor.matmul(out, k_t[:, h, c], q_t[:, h, c], start=True, stop=True)
                        else:
                            m = m_lv[h % 2][:, l - 1, win(w)]
                            last = nc.tensor.matmul(out, m, m, start=True, stop=True)
                    last.then_inc(a_done, 1)

                def kd_transposed(i):
                    h, w, n = i // TILES, i % TILES, 16 * b + i
                    if w == 0:
                        pe.wait_ge(kd_ready, 4 * b + h + 1)
                        pe.wait_ge(qe_ready, 4 * b + h + 1)
                    if not (isinstance(n, int) and n < 1):
                        pe.wait_ge(kdt_ready, n)
                    nc.tensor.transpose(ps[:, 5, 0:P], kd[:, h % 2, win(w)], ident).then_inc(kdt_done, 1)

                def outputs(i):
                    h, w, n = i // TILES, i % TILES, 16 * b + i
                    hc = win(h)
                    o = ps[:, (4, 7)[i % 2], 0:P]
                    pe.wait_ge(at_ready, n + 1)
                    if not (isinstance(n, int) and n < 2):
                        pe.wait_ge(o_squared, n - 1)
                        pe.wait_ge(o_gated, n - 1)
                    nc.tensor.matmul(o, a_t[:, i % 2, :], v_tok[:, w, hc], start=True, stop=False)
                    if not (isinstance(n, int) and n < 1):
                        pe.wait_ge(s_ready, n)
                    nc.tensor.matmul(o, qe[:, h % 2, win(w)], state[:, h, :], start=False, stop=True).then_inc(o_done, 1)
                    pe.wait_ge(kdt_ready, n + 1)
                    nc.tensor.matmul(ps[:, 6, 0:P], kd_tok[:, i % 2, :], v_tok[:, w, hc], start=True,
                                     stop=True).then_inc(su_done, 1)

                scores(0)
                scores(1)
                kd_transposed(0)
                for i in range(HEADS * TILES):
                    if i + 1 < HEADS * TILES:
                        kd_transposed(i + 1)
                    outputs(i)
                    if i + 2 < HEADS * TILES:
                        scores(i + 2)

            def head_attention():
                for h in range(HEADS):
                    hc = slice(h * P, (h + 1) * P)
                    pe.wait_ge(hops_ready, h + 1)
                    if h:
                        pe.wait_ge(hat_ready, h)
                        pe.wait_ge(hkdt_ready, h)
                    for l in range(1 + HEAD_LEVELS):
                        out = ps[0:HEAD, 0, l * HEAD:(l + 1) * HEAD]
                        if l == 0:
                            last = nc.tensor.matmul(out, k_t[:, h, 0:HEAD], q_t[:, h, 0:HEAD], start=True, stop=True)
                        else:
                            last = nc.tensor.matmul(out, h_lv[:, l - 1, :], h_lv[:, l - 1, :], start=True, stop=True)
                    last.then_inc(ha_done, 1)
                    nc.tensor.transpose(ps[0:HEAD, 5, 0:P], h_kd, ident).then_inc(hkdt_done, 1)
                    pe.wait_ge(hat_ready, h + 1)
                    pe.wait_ge(rec_state_loaded, 16 * (h + 1))
                    if h:
                        pe.wait_ge(hof_ready, h)
                    for n in range(DEC_BATCH):
                        c = N_META + n * DEC_SEQ
                        nc.tensor.matmul(ps[:, 4, c:c + DEC_SEQ], s0[:, n, :], h_qe[:, c:c + DEC_SEQ], start=n == 0,
                                         stop=False, skip_group_check=True)
                    nc.tensor.matmul(ps[:, 4, N_META:HEAD], v_tok[0:HEAD, TILES, hc], ha_t[0:HEAD, N_META:HEAD],
                                     start=False, stop=True, skip_group_check=True)
                    last = nc.tensor.matmul(ps[:, 4, 0:N_META], v_tok[0:HEAD, TILES, hc], ha_t[0:HEAD, 0:N_META],
                                            start=True, stop=True)
                    last.then_inc(hof_done, 1)
                    pe.wait_ge(hkdt_ready, h + 1)
                    pe.wait_ge(v_seq_ready, h + 1)
                    if h:
                        pe.wait_ge(hs_ready, h)
                    for n0 in range(0, SEQS, 4):
                        m = min(4, SEQS - n0)
                        last = nc.tensor.matmul(ps[:, 1 + n0 // 4, 0:m * P], kd_tok[0:HEAD, 0, :],
                                                v_seq[0:HEAD, n0:n0 + m, :], start=True, stop=True)
                    last.then_inc(hs_done, 1)
                    pe.wait_ge(hof_ready, h + 1)
                    if h:
                        pe.wait_ge(ho_squared, h)
                        pe.wait_ge(ho_gated, h)
                    nc.tensor.transpose(ps[0:HEAD, 7, 0:P], o_feat, ident).then_inc(ho_done, 1)

            def body(b, hd):
                if not hd:
                    pe.wait_ge(h_ready, 2 * (8 * b + TILES))
                    pe.wait_ge(x2_ready, 8 * b)
                for i in range(8):
                    if i in (2, 3, 4, 5):
                        pe.wait_ge(f_taken, 4 * b + i - 1)
                    if i in (6, 7):
                        pe.wait_ge(q_taken, 4 * b + i - 5)
                    feature_tile(b, i, i, i % 2, 2 + i % 2, hd)
                if hd:
                    pe.wait_ge(q_taken, 3)
                token_tiles(b, U_GATE, (4, 5, 6, 7), 2, hd)
                pe.wait_ge(q_taken, 4 * b + 4)
                if hd:
                    pe.wait_ge(gate_taken, 4 * b + 1)
                token_tiles(b, U_V, (0, 1, 2, 3), 4, hd)
                pe.wait_ge(gate_taken, 4 * b + 4)
                if hd:
                    pe.wait_ge(pool_state_loaded, 16)
                    for g in range(HEADS):
                        last = nc.tensor.transpose(ps[:, 6, g * 120:(g + 1) * 120],
                                                   pool_rows[0:120, g * P:(g + 1) * P], ident[0:120, 0:120])
                    last.then_inc(pool_in_t, 1)
                    pe.wait_ge(pool_in_taken, 1)
                for i in range(4):
                    if hd and i:
                        pe.wait_ge(u_taken, i)
                    elif i >= 2:
                        pe.wait_ge(u_taken, 4 * b + i - 1)
                    feature_tile(b, U_U + i, i, 5 + i % 2, 7, hd)
                pe.wait_ge(v_taken, 4 * b + 4)
                for g in range(HEADS):
                    pe.wait_ge(pooled_ready, 4 * b + g + 1)
                    if g >= 2 or (hd and g >= 1):
                        pe.wait_ge(pool_taken, 4 * b + g - (0 if hd else 1))
                    last = nc.tensor.matmul(ps[:, g % 2, :], wp[:, g, :], pooled[:, g, HEAD:WIDE], start=True,
                                            stop=True)
                    if hd:
                        last = nc.tensor.matmul(ps[:, 2, 0:HEAD], wp[:, g, :], pooled[:, g, 0:HEAD], start=True,
                                                stop=True)
                    last.then_inc(pool_done, 1)
                pe.wait_ge(pool_taken, 4 * b + 4)
                if hd:
                    pe.wait_ge(u_taken, 4)
                    for g in range(HEADS):
                        last = nc.tensor.transpose(ps[0:SAMPLES, 3, g * P:(g + 1) * P],
                                                   u_rows[:, g * SAMPLES:(g + 1) * SAMPLES], ident)
                    last.then_inc(u_rows_t, 1)
                    head_attention()
                    pe.wait_ge(hs_ready, HEADS)
                    pe.wait_ge(ho_squared, HEADS)
                    pe.wait_ge(ho_gated, HEADS)
                    pe.wait_ge(u_rows_ready, 1)
                attention(b)
                pe.wait_ge(a_masked, 16 * b + 16)
                for t in range(TILES):
                    pe.wait_ge(y_ready, 4 * b + t + 1)
                    if t >= 2:
                        pe.wait_ge(y_taken, 4 * b + t - 1)
                    for h in range(HEADS):
                        last = nc.tensor.transpose(ps[:, t % 2, h * P:(h + 1) * P], gate[:, t, h * P:(h + 1) * P], ident)
                    last.then_inc(yt_done, 1)
                if hd:
                    for h in range(HEADS):
                        last = nc.tensor.transpose(ps[:, 2, h * HEAD:(h + 1) * HEAD],
                                                   gate[0:HEAD, TILES, h * P:(h + 1) * P], ident[0:HEAD, 0:HEAD])
                    last.then_inc(hxt_done, 1)
                    pe.wait_ge(hh_ready, 2)
                pe.wait_ge(y_taken, 4 * b + 4)
                pe.wait_ge(o_gated, 16 * b + 16)
                pe.wait_ge(o_squared, 16 * b + 16)
                pe.wait_ge(s_ready, 16 * b + 16)
                for n in range(2):
                    if n:
                        pe.wait_ge(x1_ready, 8 * b + (2 if hd else 1))
                    token_tiles(b, U_OUT + 4 * n, [bank(n, t) for t in range(TILES)], bank(n, TILES), hd)
                norm_transposes(b, 1, hd)
                up(b, hd)
                down(b, hd)

            def up(b, hd):
                if hd:
                    pe.wait_ge(conv_state_loaded, 16)
                    for f in range(FT):
                        last = nc.tensor.transpose(ps[:, 6, f * 16:(f + 1) * 16], conv_rows[0:16, f * P:(f + 1) * P],
                                                   ident[0:16, 0:16])
                    last.then_inc(conv_in_t, 1)

                def pair(j, first):
                    for r in range(2):
                        n = FT * b + 2 * j + r
                        u = UNITS * b + U_UP + 4 * j + 2 * r
                        pe.wait_ge(w_ready, u + 1)
                        if not first:
                            pe.wait_ge(a_taken, n - 1)
                            if hd:
                                pe.wait_ge(hb_taken, n - 1)
                        last = features(2 * r, ps[:, r, :], MAIN)
                        if hd:
                            last = features(2 * r, ps[:, 4 + r, 0:HEAD], slice(0, HEAD))
                        last.then_inc(unit_done, 1)
                        pe.wait_ge(w_ready, u + 2)
                        if not first:
                            pe.wait_ge(act_ready, n - 1)
                        last = features(2 * r + 1, ps[:, 2 + r, :], MAIN)
                        if hd:
                            pe.wait_ge(ha_taken, n + 1)
                            last = features(2 * r + 1, ps[:, 4 + r, 64:64 + HEAD], slice(0, HEAD))
                        last.then_inc(unit_done, 1)

                pair(0, True)
                with pe.Fori(1, FT // 2) as j:
                    pair(j, False)
                if hd:
                    pe.wait_ge(hb_taken, FT)
                    for half in range(2):
                        if half:
                            pe.wait_ge(conv_out_taken, 1)
                        for f in range(11 * half, 11 * half + 11):
                            last = nc.tensor.transpose(ps[0:16, 5 + (f % 11) // 4, (f % 11 % 4) * P:(f % 11 % 4 + 1) * P],
                                                       conv_out[:, f, :], ident)
                        last.then_inc(conv_out_t, 1)
                    pe.wait_ge(conv_out_taken, 2)

            def down(b, hd):
                for n in range(2):
                    def ktile(i, kk, slot, wk, first, fin):
                        d = 2 * FT * b + FT * n + 2 * i + kk
                        pe.wait_ge(act_lo_ready, d + 1)
                        for t in range(TILES + hd):
                            cols = main(t) if t < TILES else slice(0, HEAD)
                            out = ps[:, bank(n, t), :] if t < TILES else ps[0:HEAD, bank(n, t), :]
                            last = three(out, (act_hi[:, kk, cols], act_lo[:, kk, cols]),
                                         [w[:, slot, wk * 512:(wk + 1) * 512] for w in (w_hi, w_lo)], first, fin)
                        return last

                    def pair(i, slot, first):
                        pe.wait_ge(w_ready, UNITS * b + U_DOWN + 12 * n + i + 1)
                        ktile(i, 0, slot, 0, first, False).then_inc(act0_used, 1)
                        ktile(i, 1, slot, 1, False, False).then_inc(unit_done, 1)

                    if n:
                        pe.wait_ge(x2_ready, 8 * b + (2 if hd else 1))
                    pair(0, 0, True)
                    if n:
                        for i in range(1, NEXT_AT):
                            pair(i, i % 4, False)
                        for t in range(TILES):
                            pair(NEXT_AT + t, (NEXT_AT + t) % 4, False)
                            if t == 0:
                                pe.wait_ge(x2_ready, 8 * b + 4)
                            row_transposes(8 * b + 8, t, 2, 1)
                    with pe.Fori(NEXT_AT + TILES if n else 1, 10) as i:
                        pair(i, i % 4, False)
                    for kk in range(2):
                        pe.wait_ge(w_ready, UNITS * b + U_DOWN + 12 * n + 10 + kk + 1)
                        ktile(10, kk, 2 + kk, kk, False, kk == 1).then_inc(unit_done, 1)

            pe.wait_ge(tab_loaded, 16)
            pe.wait_ge(vec_loaded, 16)
            nc.tensor.transpose(ps[:, 0, 0:V_END], junk[0:V_END, 0:P], ident[0:V_END, 0:V_END]).then_inc(setup_t, 1)
            pe.wait_ge(setup_done, 1)
            pe.wait_ge(small_loaded, 48)
            norm_transposes(0, 0, 1)
            body(0, 1)
            with pe.Fori(1, BLOCKS) as b:
                body(b, 0)
            pe.wait_ge(x2_ready, 8 * BLOCKS)
            for g in range(HEADS):
                last = nc.tensor.transpose(ps[0:POOL_BUF, 0, g * P:(g + 1) * P], u_hist[:, g, :], ident)
            last.then_inc(last_t, 1)
            for f in range(FT):
                last = nc.tensor.transpose(ps[0:2, 1 + f // 4, (f % 4) * P:(f % 4 + 1) * P], conv_hist[:, f, :], ident)
            last.then_inc(last_t, 1)

        @block.scalar
        def _(act):
            own = Order(act, act_order)

            def square(x, t, n):
                if not (isinstance(n, int) and n == 0):
                    act.wait_ge(squared, n)
                nc.scalar.activation(junk, x[:, t, :], ACT.Square, accum_out=sumsq[:, t:t + 1]).then_inc(squared, 1)

            def squares(b, w, hd):
                n = (0, 12 * b + 4, 12 * b + 12)[w]
                if w:
                    act.wait_ge(hsquared, w if hd else 3)
                for t in range(TILES):
                    if w == 0:
                        act.wait_ge(x_loaded[t], 16)
                    elif w == 1:
                        act.wait_ge(x1_ready, 8 * b + 4 + t + 1)
                    else:
                        act.wait_ge(x2_ready, 8 * b + 4 + t + 1)
                    square(x_tok, t, n + t)
                if hd:
                    if w == 0:
                        act.wait_ge(hx_loaded, 32)
                    else:
                        act.wait_ge((hx1_ready, hx2_ready)[w - 1], 2)
                    act.wait_ge(squared, n + TILES)
                    nc.scalar.activation(junk[0:HEAD, :], x_tok[0:HEAD, TILES, :], ACT.Square,
                                         accum_out=sumsq[0:HEAD, TILES:TILES + 1]).then_inc(hsquared, 1)

            def root_guess(v, out, ready, value, signal):
                act.wait_ge(ready, value)
                own.mark(nc.scalar.activation(out, v, ACT.Ln))
                own.settle()
                nc.scalar.activation(out, out, ACT.Exp, scale=-0.5).then_inc(signal, 1)

            def rows_hi(n, t):
                for half in range(2):
                    act.wait_ge(t32_ready, 2 * (n + t) + half + 1)
                    nc.scalar.copy(h_hi[:, 4 * half:4 * half + 4, main(t)],
                                   t32[:, half, :].rearrange("p (k n) -> p k n", k=4)).then_inc(h_hi_ready, 1)

            def norm_hi(b, w, hd):
                for t in range(TILES):
                    rows_hi(8 * b + 4 * w, t)
                if hd:
                    act.wait_ge(ht32_ready, w + 1)
                    nc.scalar.copy(h_hi[:, :, 0:HEAD], t32[:, 0, 0:KD * HEAD].rearrange("p (k n) -> p k n", k=KD)
                                   ).then_inc(hh_hi_ready, 1)

            def decays(b, h, steps):
                for i in steps:
                    act.wait_ge(dec_ready, 8 * (4 * b + h) + i + 1)
                    nc.scalar.activation(dec[:, i % 2, :], dec[:, i % 2, :], ACT.Exp).then_inc(dec_exp, 1)
                    if i == LEVELS:
                        g = g_t[:, h, HEAD:WIDE]
                        if not (isinstance(b, int) and h == 0):
                            act.wait_ge(s_ready, 16 * b if h < 2 else 16 * b + 4 * (h - 1))
                        nc.scalar.activation(g_end[:, h, :], g.rearrange("p (w t) -> p w t", t=P)[:, :, P - 1],
                                             ACT.Exp)
                        nc.scalar.activation(qe[:, h % 2, :], g, ACT.Exp).then_inc(eg_ready, 1)

            def body(b, hd):
                lo = 0 if hd else HEAD
                for h in range(HEADS):
                    act.wait_ge(f_taken, 4 * b + h + 1)
                    nc.scalar.activation(f_u[:, h % 2, lo:WIDE], f_u[:, h % 2, lo:WIDE], ACT.Exp, scale=-1.0).then_inc(
                        f_exp, 1)
                    act.wait_ge(f_sig, 4 * b + h + 1)
                    nc.scalar.activation(f_u[:, h % 2, lo:WIDE], f_u[:, h % 2, lo:WIDE], ACT.Ln).then_inc(f_ln, 1)
                for h in range(HEADS):
                    act.wait_ge(unit_done, UNITS * b + U_Q + h + 1)
                    if hd:
                        nc.scalar.activation(q_t[:, h, 0:HEAD], ps[:, 2 + h % 2, 0:HEAD], ACT.Silu)
                    nc.scalar.activation(q_t[:, h, HEAD:WIDE], ps[:, h % 2, :], ACT.Silu).then_inc(q_taken, 1)
                nc.scalar.preload_act_table_set("natural_log_exp_and_others")
                for h in range(1 if hd else 2):
                    decays(b, h, range(1 + LEVELS))
                nc.scalar.preload_act_table(ACT.Silu)
                act.wait_ge(unit_done, UNITS * b + U_GATE + 4)
                if hd:
                    nc.scalar.activation(gate[0:HEAD, TILES, :], ps[0:HEAD, 2, :], ACT.Silu)
                for t in range(TILES):
                    nc.scalar.activation(gate[:, t, :], ps[:, 4 + t, :], ACT.Silu).then_inc(gate_taken, 1)
                nc.scalar.preload_act_table_set("natural_log_exp_and_others")
                act.wait_ge(unit_done, UNITS * b + U_V + 4)
                if hd:
                    nc.scalar.copy(v_tok[0:HEAD, TILES, :], ps[0:HEAD, 4, :])
                for t in range(TILES):
                    nc.scalar.copy(v_tok[:, t, :], ps[:, t, :]).then_inc(v_taken, 1)
                if hd:
                    act.wait_ge(pool_in_taken, 1)
                for g in range(HEADS):
                    act.wait_ge(unit_done, UNITS * b + U_U + g + 1)
                    if g >= 2:
                        act.wait_ge(pooled_ready, 4 * b + g - 1)
                    act.wait_ge(g_ready, 4 * b + HEADS)
                    if hd:
                        if g:
                            act.wait_ge(pooled_ready, g)
                        he = hu_ext
                        nc.scalar.copy(he[:, 0, POOL_BUF:EXT], ps[:, 7, 0:N_META])
                        nc.scalar.copy(he[:, 1:SEQS, POOL_BUF:POOL_BUF + DEC_SEQ],
                                       ps[:, 7, N_META:HEAD].rearrange("p (n t) -> p n t", t=DEC_SEQ))
                        nc.scalar.copy(u_rows[:, g * SAMPLES:(g + 1) * SAMPLES], ps[:, 7, N_META:HEAD])
                    nc.scalar.copy(u_ext[:, g % 2, POOL_BUF:POOL_BUF + BLOCK], ps[:, 5 + g % 2, :]).then_inc(u_taken, 1)
                for g in range(HEADS):
                    act.wait_ge(pool_done, 4 * b + g + 1)
                    sc = vec[:, V_SCALE + g:V_SCALE + g + 1]
                    if hd:
                        nc.scalar.activation(h_hi[:, g, 0:HEAD], ps[:, 2, 0:HEAD], ACT.Copy, scale=sc)
                    nc.scalar.activation(h_hi[:, g, HEAD:WIDE], ps[:, g % 2, :], ACT.Copy, scale=sc).then_inc(pool_hi, 1)
                if hd:
                    act.wait_ge(u_rows_t, 1)
                    act.wait_ge(pool_taken, 4)
                    nc.scalar.copy(pool_rows[0:SAMPLES, :], ps[0:SAMPLES, 3, :]).then_inc(u_rows_ready, 1)
                    act.wait_ge(u_rows_ready, 1)
                    act.dma_start(pool_sample[:, POOL_BUF - DEC_SEQ:POOL_BUF, :], pool_rows[0:SAMPLES, :]).then_inc(
                        u_rows_ready, 16)
                    for h in range(HEADS):
                        if h:
                            act.wait_ge(rec_stored, 16 * h)
                        else:
                            act.wait_ge(pooled_ready, 4)
                            act.wait_ge(pool_done, 4)
                            act.wait_ge(u_rows_ready, 17)
                        act.dma_start(s0, state_rec[:, h].rearrange("n d v -> d n v")).then_inc(rec_state_loaded, 16)
                        act.wait_ge(hdec_ready, h + 1)
                        nc.scalar.activation(h_dec[:, :, :], h_dec[:, :, :], ACT.Exp).then_inc(hdec_exp, 1)
                        act.wait_ge(hkdt_done, h + 1)
                        nc.scalar.copy(kd_tok[0:HEAD, 0, :], ps[0:HEAD, 5, 0:P]).then_inc(hkdt_ready, 1)
                        act.wait_ge(hof_done, h + 1)
                        nc.scalar.copy(o_feat, ps[:, 4, 0:HEAD]).then_inc(hof_ready, 1)
                        act.wait_ge(ho_done, h + 1)
                        if h:
                            act.wait_ge(ho_squared, h)
                        nc.scalar.activation(o_junk[0:HEAD, :], ps[0:HEAD, 7, 0:P], ACT.Square,
                                             accum_out=osumsq[0:HEAD, TILES, h:h + 1]).then_inc(ho_squared, 1)
                        act.wait_ge(hs_ready, h + 1)
                        act.dma_start(rec_sample[:, h].rearrange("n d v -> d n v"), s0).then_inc(rec_stored, 16)
                    act.wait_ge(rec_stored, 16 * HEADS)
                    act.wait_ge(ho_squared, HEADS)
                if hd:
                    decays(b, 1, range(1 + LEVELS))
                for i in range(HEADS * TILES):
                    h, w, n = i // TILES, i % TILES, 16 * b + i
                    act.wait_ge(kdt_done, n + 1)
                    if not (isinstance(n, int) and n < 2):
                        act.wait_ge(su_done, n - 1)
                    nc.scalar.copy(kd_tok[:, i % 2, :], ps[:, 5, 0:P]).then_inc(kdt_ready, 1)
                    act.wait_ge(o_done, n + 1)
                    if not (isinstance(n, int) and n == 0):
                        act.wait_ge(o_squared, n)
                    nc.scalar.activation(o_junk[:, :], ps[:, (4, 7)[i % 2], 0:P], ACT.Square,
                                         accum_out=osumsq[:, w, h:h + 1]).then_inc(o_squared, 1)
                    if i in AHEAD:
                        decays(b, *AHEAD[i])
                root_guess(ovar[:, :], orstd[:, :], ovar_ready, b + 1, oguess_ready)
                for t in range(TILES):
                    act.wait_ge(yt_done, 4 * b + t + 1)
                    nc.scalar.copy(h_hi[:, 4:8, main(t)], ps[:, t % 2, :].rearrange("p (k n) -> p k n", k=4)).then_inc(
                        y_hi, 1)
                if hd:
                    act.wait_ge(hxt_done, 2)
                    nc.scalar.copy(h_hi[:, 4:8, 0:HEAD], ps[:, 2, 0:4 * HEAD].rearrange("p (k n) -> p k n", k=4)
                                   ).then_inc(hh_hi_ready, 1)
                squares(b, 1, hd)
                root_guess(var[:, :], rstd[:, :], var_ready, 3 * b + 2, guess_ready)
                norm_hi(b, 1, hd)
                if hd:
                    act.dma_start(conv_rows[0:16, :], state_conv.rearrange("n r f -> (n r) f")).then_inc(
                        conv_state_loaded, 16)
                nc.scalar.preload_act_table(ACT.Gelu)

                def up_tile(j, r, first):
                    n = FT * b + 2 * j + r
                    ft = 2 * j + r
                    bias = vec[:, bass.ds(V_CONV_B + ft, 1)]
                    w2 = vec[:, bass.ds(V_CONV_W + 2 * FT + ft, 1)]
                    act.wait_ge(unit_done, UNITS * b + U_UP + 4 * j + 2 * r + 1)
                    if not first:
                        act.wait_ge(act_ready, n - 1)
                    if hd:
                        hae = ha_ext[:, r, :].rearrange("p (n t) -> p n t", n=SEQS)
                        hcv = hconv[:, r, :].rearrange("p (n t) -> p n t", n=SEQS)
                        if not first:
                            act.wait_ge(hb_taken, n - 1)
                        act.wait_ge(hist_ready, n + 1)
                        nc.scalar.copy(hae[:, 0, 2:2 + N_META], ps[:, 4 + r, 0:N_META])
                        own.mark(nc.scalar.copy(hae[:, 1:SEQS, 2:2 + DEC_SEQ],
                                                ps[:, 4 + r, N_META:HEAD].rearrange("p (n t) -> p n t", t=DEC_SEQ)))
                        own.settle()
                        nc.scalar.activation(hcv, hae[:, :, 2:2 + N_META], ACT.Identity, bias=bias, scale=w2).then_inc(
                            ha_taken, 1)
                    nc.scalar.copy(a_ext[:, r, 2:2 + BLOCK], ps[:, r, :])
                    nc.scalar.activation(conv[:, r, :], ps[:, r, :], ACT.Identity, bias=bias, scale=w2).then_inc(
                        a_taken, 1)
                    if hd:
                        act.wait_ge(hconv_ready, n + 1)
                        nc.scalar.activation(hcv, hcv, ACT.Gelu).then_inc(hgelu_ready, 1)
                    act.wait_ge(conv_ready, n + 1)
                    nc.scalar.activation(gelu[:, r, :], conv[:, r, :], ACT.Gelu).then_inc(gelu_ready, 1)

                for r in range(2):
                    up_tile(0, r, True)
                with own.loop(1, FT // 2, 2 if hd else 0) as j:
                    for r in range(2):
                        up_tile(j, r, False)
                if hd:
                    for half in range(2):
                        act.wait_ge(conv_out_t, half + 1)
                        for i in range(3):
                            m = (4, 4, 3)[i] * P
                            at = (11 * half + 4 * i) * P
                            last = nc.scalar.copy(conv_rows[0:16, at:at + m], ps[0:16, 5 + i, 0:m])
                        last.then_inc(conv_out_taken, 1)
                    act.wait_ge(conv_out_taken, 2)
                    act.dma_start(conv_sample.rearrange("n r f -> (n r) f"), conv_rows[0:16, :]).then_inc(
                        conv_out_taken, 16)
                    act.wait_ge(conv_out_taken, 18)
                def split(n, i, kk, first):
                    u = UNITS * b + U_DOWN + 12 * n
                    if not first:
                        if kk == 0:
                            act.wait_ge(act0_used, 20 * b + 10 * n + i)
                        else:
                            act.wait_ge(unit_done, u + i)
                    elif n:
                        act.wait_ge(unit_done, u - 1 + kk)
                    elif kk == 0:
                        act.wait_ge(act_ready, FT * (b + 1))
                        if hd:
                            act.wait_ge(hb_taken, FT)
                    lo = 0 if hd else HEAD
                    nc.scalar.copy(act_hi[:, kk, lo:WIDE],
                                   acts[:, bass.ds(2 * i + kk, 1), lo:WIDE].rearrange("p a b -> p (a b)")).then_inc(
                                       act_hi_ready, 1)

                def pair(n, i, first=False):
                    for kk in range(2):
                        split(n, i, kk, first)

                pair(0, 0, True)
                with act.Fori(1, 5) as i:
                    pair(0, i)
                for t in range(TILES):
                    pair(0, 5 + t)
                    act.wait_ge(x_next_loaded[t], 16 * (b + 1))
                    square(x_next, t, 12 * b + 8 + t)
                for i in range(9, FT // 2):
                    pair(0, i)
                nc.scalar.preload_act_table_set("natural_log_exp_and_others")
                pair(1, 0, True)
                root_guess(var[:, :], rstd[:, :], var_ready, 3 * b + 3, guess_ready)
                for i in range(1, NEXT_AT + 1):
                    pair(1, i)
                for t in range(TILES):
                    pair(1, NEXT_AT + 1 + t)
                    rows_hi(8 * b + 8, t)
                with act.Fori(NEXT_AT + 1 + TILES, FT // 2) as i:
                    pair(1, i)
                squares(b, 2, hd)
                root_guess(var[:, :], rstd[:, :], var_ready, 3 * b + 4, guess_ready)
                if hd:
                    act.wait_ge(hout_ready, 1)
                    act.dma_start(y_sample, x_tok[N_META:HEAD, TILES, :]).then_inc(hout_ready, 16)

            act.wait_ge(vec_ready, 1)
            nc.scalar.preload_act_table_set("natural_log_exp_and_others")
            nc.scalar.activation(lb[:, 0, :], lb[:, 0, :], ACT.Exp).then_inc(lb_exp, 1)
            act.wait_ge(setup_done, 1)
            squares(0, 0, 1)
            root_guess(var[:, :], rstd[:, :], var_ready, 1, guess_ready)
            norm_hi(0, 0, 1)
            body(0, 1)
            with own.loop(1, BLOCKS, 4) as b:
                body(b, 0)
            act.wait_ge(last_t, 1)
            nc.scalar.copy(last_rows[0:POOL_BUF, :], ps[0:POOL_BUF, 0, :]).then_inc(last_taken, 1)
            act.wait_ge(last_t, 2)
            for i in range(6):
                m = min(4, FT - 4 * i) * P
                last = nc.scalar.copy(conv_rows[0:2, 4 * i * P:4 * i * P + m], ps[0:2, 1 + i, 0:m])
            last.then_inc(last_taken, 1)
            act.wait_ge(u_rows_ready, 17)
            act.wait_ge(hout_ready, 17)
            act.wait_ge(rec_stored, 16 * HEADS)

        @block.vector
        def _(dve):
            own = Order(dve, dve_order)
            v = nc.vector

            def root(x, y, t, mean, ready, value, guess, gvalue, src):
                own.settle()
                v.tensor_scalar(x, src, mean, EPS, ALU.mult, ALU.add).then_inc(ready, 1)
                root_step(x, y, t, guess, gvalue)

            def root_step(x, y, t, guess, gvalue):
                dve.wait_ge(guess, gvalue)
                own.mark(v.tensor_tensor(t, y, y, ALU.mult))
                own.settle()
                own.mark(v.tensor_tensor(t, t, x, ALU.mult))
                own.settle()
                own.mark(v.tensor_scalar(t, t, -0.5, 1.5, ALU.mult, ALU.add))
                own.settle()
                own.mark(v.tensor_tensor(y, y, t, ALU.mult))
                own.settle()

            def scaled(n, x, t):
                if t >= 2:
                    dve.wait_ge(xt_done, 2 * (n + t - 1))
                v.tensor_scalar(xn[:, t % 2, :], x[:, t, :], rstd[:, t:t + 1], None, ALU.mult).then_inc(xn_ready, 1)

            def rows(n, w, x, t, bank0):
                for half in range(2):
                    dve.wait_ge(xt_done, 2 * (n + t) + half + 1)
                    if t:
                        dve.wait_ge(h_ready, 2 * (n + t - 1) + half + 1)
                    v.tensor_tensor(t32[:, half, :].rearrange("p (k n) -> p k n", k=4),
                                    ps[:, bank0 + half, :].rearrange("p (k n) -> p k n", k=4),
                                    gain[w][:, 4 * half:4 * half + 4].unsqueeze(2).broadcast_to([P, 4, P]),
                                    ALU.mult).then_inc(t32_ready, 1)
                if t + 2 < TILES:
                    scaled(n, x, t + 2)
                for half in range(2):
                    dve.wait_ge(h_hi_ready, 2 * (n + t) + half + 1)
                    v.tensor_tensor(h_lo[:, 4 * half:4 * half + 4, main(t)],
                                    t32[:, half, :].rearrange("p (k n) -> p k n", k=4),
                                    h_hi[:, 4 * half:4 * half + 4, main(t)].bitcast(F32),
                                    ALU.subtract).then_inc(h_ready, 1)

            def norm(b, w, hd):
                n = 8 * b + 4 * w
                dve.wait_ge(squared, 12 * b + 4 * w + TILES)
                if hd:
                    dve.wait_ge(hsquared, w + 1)
                root(var[:, :], rstd[:, :], rtmp[:, :], 1.0 / D_MODEL, var_ready, 3 * b + w + 1, guess_ready,
                     3 * b + w + 1, sumsq[:, :])
                scaled(n, x_tok, 0)
                scaled(n, x_tok, 1)
                for t in range(TILES):
                    rows(n, w, x_tok, t, 2 * (t % 2))
                if hd:
                    x = 3 if w else 1
                    v.tensor_scalar(xn[0:HEAD, 0, :], x_tok[0:HEAD, TILES, :], rstd[0:HEAD, TILES:TILES + 1], None,
                                    ALU.mult).then_inc(hxn_ready, 1)
                    dve.wait_ge(hxt_done, x)
                    dve.wait_ge(h_ready, 2 * (n + TILES))
                    th = t32[:, 0, 0:KD * HEAD].rearrange("p (k n) -> p k n", k=KD)
                    v.tensor_tensor(th, ps[:, 4, 0:KD * HEAD].rearrange("p (k n) -> p k n", k=KD),
                                    gain[w].unsqueeze(2).broadcast_to([P, KD, HEAD]), ALU.mult).then_inc(ht32_ready, 1)
                    dve.wait_ge(hh_hi_ready, x)
                    v.tensor_tensor(h_lo[:, :, 0:HEAD], th, h_hi[:, :, 0:HEAD].bitcast(F32), ALU.subtract).then_inc(
                        hh_ready, 1)

            def forget_gates(b, hd):
                lo = 0 if hd else HEAD
                c = slice(lo, WIDE)

                def clamp(h):
                    dve.wait_ge(unit_done, UNITS * b + U_F + h + 1)
                    if hd:
                        z = ps[:, 2 + h % 2, 0:HEAD]
                        v.tensor_scalar(f_u[:, h % 2, 0:HEAD], z, -40.0, None, ALU.max)
                        v.tensor_scalar(f_low[:, h % 2, 0:HEAD], z, 40.0, 0.0, ALU.add, ALU.min)
                    z = ps[:, h % 2, :]
                    v.tensor_scalar(f_u[:, h % 2, HEAD:WIDE], z, -40.0, None, ALU.max)
                    v.tensor_scalar(f_low[:, h % 2, HEAD:WIDE], z, 40.0, 0.0, ALU.add, ALU.min).then_inc(f_taken, 1)

                def gates(h):
                    u = f_u[:, h % 2, c]
                    rest = lb[:, 1, h:h + 1]
                    dve.wait_ge(f_exp, 4 * b + h + 1)
                    own.mark(v.tensor_scalar(f_r[:, c], u, 1.0, None, ALU.add))
                    own.settle()
                    own.mark(v.reciprocal(f_r[:, c], f_r[:, c]))
                    own.settle()
                    own.mark(v.scalar_tensor_tensor(out=k_t[:, h, c], in0=u, scalar=rest, in1=f_r[:, c],
                                                    op0=ALU.mult, op1=ALU.mult))
                    own.settle()
                    v.tensor_scalar(u, f_r[:, c], rest, lb[:, 0, h:h + 1], ALU.mult, ALU.add).then_inc(f_sig, 1)

                def cumulate(h):
                    dve.wait_ge(f_ln, 4 * b + h + 1)
                    low = f_low[:, h % 2, c]
                    own.mark(v.scalar_tensor_tensor(out=low, in0=low, scalar=lb[:, 2, h:h + 1], in1=f_u[:, h % 2, c],
                                                    op0=ALU.mult, op1=ALU.add))
                    own.settle()
                    v.tensor_tensor_scan(g_t[:, h, c], reset[:, c], low, 0.0, ALU.mult, ALU.add).then_inc(g_ready, 1)

                clamp(0)
                for h in range(HEADS):
                    gates(h)
                    if h + 1 < HEADS:
                        if h:
                            dve.wait_ge(g_ready, 4 * b + h)
                        clamp(h + 1)
                    cumulate(h)

            def window_sums(src, bufs, size, g, dims):
                now, shift = src, 1
                for i in range(g + 1):
                    nxt = bufs[i % 2]
                    if i:
                        own.settle()
                    start = 2 * shift - 1
                    own.mark(v.tensor_tensor(dims(nxt, start, size), dims(now, start, size),
                                             dims(now, start - shift, size - shift), ALU.add))
                    now, shift = nxt, 2 * shift
                own.settle()
                return now

            def pool_branch(b, hd):
                if hd:
                    dve.wait_ge(pool_in_t, 1)
                    dve.wait_ge(g_ready, 4)
                    own.mark(v.memset(hu_ext, 0.0))
                    own.mark(v.memset(hu_sum[:, :, :], 0.0))
                    own.settle()
                    v.tensor_copy(pool_in, ps[:, 6, 0:480]).then_inc(pool_in_taken, 1)
                def low_part(g):
                    dve.wait_ge(pool_hi, 4 * b + g + 1)
                    sc = vec[:, V_SCALE + g:V_SCALE + g + 1]
                    if hd:
                        v.scalar_tensor_tensor(out=h_lo[:, g, 0:HEAD], in0=ps[:, 2, 0:HEAD], scalar=sc,
                                               in1=h_hi[:, g, 0:HEAD].bitcast(F32), op0=ALU.mult, op1=ALU.subtract)
                    v.scalar_tensor_tensor(out=h_lo[:, g, HEAD:WIDE], in0=ps[:, g % 2, :], scalar=sc,
                                           in1=h_hi[:, g, HEAD:WIDE].bitcast(F32), op0=ALU.mult,
                                           op1=ALU.subtract).then_inc(pool_taken, 1)

                for g in range(HEADS):
                    w = WINDOWS[g]
                    if hd:
                        dve.wait_ge(pool_in_taken, 1)
                        if g:
                            own.settle()
                            dve.wait_ge(pooled_ready, g)
                        own.mark(v.tensor_copy(
                            hu_ext[:, 1:SEQS, 0:POOL_BUF],
                            pool_in[:, g * 120:(g + 1) * 120].rearrange("p (n t) -> p n t", t=POOL_BUF)))
                        own.settle()
                    dve.wait_ge(u_taken, 4 * b + g + 1)
                    if hd:
                        own.mark(v.tensor_copy(u_hist[:, g, :], hu_ext[:, 0, EXT - POOL_BUF:EXT]))
                        own.settle()

                        def hview(t, a, z):
                            t = t if len(t.shape) == 3 else t.rearrange("p (n t) -> p n t", n=SEQS)
                            return t[:, :, a:z]
                        s = window_sums(hu_ext, (hu_sum[:, 0, :], hu_sum[:, 1, :]), EXT, g, hview)
                        s = s.rearrange("p (n t) -> p n t", n=SEQS)
                        own.mark(v.tensor_tensor(s[:, 0, POOL_BUF:EXT], s[:, 0, POOL_BUF:EXT],
                                                 tab[:, C_COUNT + g * N_META:C_COUNT + (g + 1) * N_META], ALU.mult))
                        own.settle()
                        v.tensor_tensor(pooled[:, g, 0:N_META], s[:, 0, POOL_BUF:EXT], hu_ext[:, 0, POOL_BUF:EXT],
                                        ALU.subtract)
                        v.scalar_tensor_tensor(
                            out=pooled[:, g, N_META:HEAD].rearrange("p (n t) -> p n t", t=DEC_SEQ),
                            in0=s[:, 1:SEQS, POOL_BUF:POOL_BUF + DEC_SEQ], scalar=1.0 / w,
                            in1=hu_ext[:, 1:SEQS, POOL_BUF:POOL_BUF + DEC_SEQ], op0=ALU.mult, op1=ALU.subtract)
                    ue = u_ext[:, g % 2, :]
                    own.mark(v.tensor_copy(ue[:, 0:POOL_BUF], u_hist[:, g, :]))
                    own.settle()
                    own.mark(v.tensor_copy(u_hist[:, g, :], ue[:, BLOCK:BLOCK + POOL_BUF]))
                    s = window_sums(ue, (u_sum[:, 0, :], u_sum[:, 1, :]), POOL_BUF + BLOCK, g, lambda t, a, z: t[:, a:z])
                    v.scalar_tensor_tensor(out=pooled[:, g, HEAD:WIDE], in0=s[:, POOL_BUF:POOL_BUF + BLOCK],
                                           scalar=1.0 / w, in1=ue[:, POOL_BUF:POOL_BUF + BLOCK], op0=ALU.mult,
                                           op1=ALU.subtract).then_inc(pooled_ready, 1)
                for g in range(HEADS):
                    low_part(g)

            def head_attention():
                dve.wait_ge(v_taken, 4)
                dve.wait_ge(q_taken, 4)
                dve.wait_ge(g_ready, 4)
                dve.wait_ge(u_rows_ready, 17)
                own.mark(v.memset(h_lv[:, :, :], 0.0))
                own.mark(v.memset(h_dec[:, :, :], 0.0))
                own.settle()
                for h in range(HEADS):
                    g = g_t[:, h, 0:HEAD]
                    gs = g[:, N_META:HEAD].rearrange("p (n t) -> p n t", t=DEC_SEQ)
                    q, k = q_t[:, h, 0:HEAD], k_t[:, h, 0:HEAD]
                    if h:
                        dve.wait_ge(hs_done, h)
                        dve.wait_ge(hs_ready, h)
                    v.tensor_tensor(h_dec[:, 0, 0:N_META], g[:, N_META - 1:N_META].broadcast_to([P, N_META]),
                                    g[:, 0:N_META], ALU.subtract)
                    v.tensor_tensor(h_dec[:, 0, N_META:HEAD].rearrange("p (n t) -> p n t", t=DEC_SEQ),
                                    gs[:, :, DEC_SEQ - 1:DEC_SEQ].broadcast_to([P, DEC_BATCH, DEC_SEQ]), gs,
                                    ALU.subtract)
                    last = v.tensor_copy(h_dec[:, 1, :], g)
                    for l in range(HEAD_LEVELS):
                        last = exponents(h_dec[:, 2 + l, :], g, 2 ** l, HEAD if 2 ** l < DEC_SEQ else N_META)
                    last.then_inc(hdec_ready, 1)
                    dve.wait_ge(hdec_exp, h + 1)
                    v.tensor_tensor(h_kd, k, h_dec[:, 0, :], ALU.mult)
                    v.scalar_tensor_tensor(out=h_qe, in0=q, scalar=Q_SCALE, in1=h_dec[:, 1, :], op0=ALU.mult,
                                           op1=ALU.mult)
                    for l in range(HEAD_LEVELS):
                        last = level_operand(h_lv[:, l, :], h_dec[:, 2 + l, :], k, q, 2 ** l,
                                             HEAD if 2 ** l < DEC_SEQ else N_META)
                    last.then_inc(hops_ready, 1)
                    v.tensor_tensor(v_seq[0:HEAD, :, :],
                                    v_tok[0:HEAD, TILES, h * P:(h + 1) * P].unsqueeze(1).broadcast_to([HEAD, SEQS, P]),
                                    tab[0:HEAD, C_SEQ:C_SEQ + SEQS].unsqueeze(2).broadcast_to([HEAD, SEQS, P]),
                                    ALU.mult).then_inc(v_seq_ready, 1)
                    dve.wait_ge(ha_done, h + 1)
                    own.mark(v.tensor_tensor(ha_all[0:HEAD, :], ps[0:HEAD, 0, 0:(1 + HEAD_LEVELS) * HEAD], hmasks,
                                             ALU.mult))
                    own.settle()
                    v.tensor_reduce(ha_t[0:HEAD, :], ha_all[0:HEAD, :].rearrange("p (l t) -> p t l", t=HEAD),
                                    mybir.AxisListType.X, ALU.add).then_inc(hat_ready, 1)
                    dve.wait_ge(ho_squared, h + 1)
                    gt = gate[0:HEAD, TILES, h * P:(h + 1) * P]
                    v.tensor_tensor(gt, gt, ps[0:HEAD, 7, 0:P], ALU.mult).then_inc(ho_gated, 1)
                    dve.wait_ge(hs_done, h + 1)
                    v.tensor_copy(state[:, h, :], ps[:, 1, 0:P])
                    for n in range(DEC_BATCH):
                        c = N_META + n * DEC_SEQ + DEC_SEQ - 1
                        i = n + 1
                        last = v.scalar_tensor_tensor(out=s0[:, n, :], in0=s0[:, n, :], scalar=h_dec[:, 1, c:c + 1],
                                                      in1=ps[:, 1 + i // 4, (i % 4) * P:(i % 4 + 1) * P], op0=ALU.mult,
                                                      op1=ALU.add)
                    last.then_inc(hs_ready, 1)

            def exponents(out, g, half, size):
                o = out[:, 0:size].rearrange("p (n t) -> p n t", t=2 * half)
                gg = g[:, 0:size].rearrange("p (n t) -> p n t", t=2 * half)
                bb = gg[:, :, half - 1:half].broadcast_to([P, size // (2 * half), half])
                v.tensor_tensor(o[:, :, 0:half], bb, gg[:, :, 0:half], ALU.subtract)
                return v.tensor_tensor(o[:, :, half:2 * half], gg[:, :, half:2 * half], bb, ALU.subtract)

            def level_operand(out, e, k, q, half, size):
                def halves(t):
                    t = t[:, 0:size].rearrange("p (n t) -> p n t", t=2 * half)
                    return t[:, :, 0:half], t[:, :, half:2 * half]
                (ol, orr), (el, er) = halves(out), halves(e)
                v.tensor_tensor(ol, halves(k)[0], el, ALU.mult)
                return v.tensor_tensor(orr, halves(q)[1], er, ALU.mult)

            def exponent(b, h, i):
                g = g_t[:, h, HEAD:WIDE]
                if i == 1:
                    if not (isinstance(b, int) and h == 0):
                        dve.wait_ge(kd_ready, 4 * b + h)
                elif not (isinstance(b, int) and h == 0 and i == 0):
                    dve.wait_ge(lv_ready, LEVELS * (4 * b + h) + max(i - 1, 0))
                if i == LEVELS:
                    gw = g.rearrange("p (w t) -> p w t", t=P)
                    v.tensor_tensor(dec[:, i % 2, :].rearrange("p (w t) -> p w t", t=P),
                                    gw[:, :, P - 1:P].broadcast_to([P, TILES, P]), gw, ALU.subtract).then_inc(dec_ready, 1)
                else:
                    exponents(dec[:, i % 2, :], g, 2 ** i, BLOCK).then_inc(dec_ready, 1)

            def operand(b, h, i):
                q, k = q_t[:, h, HEAD:WIDE], k_t[:, h, HEAD:WIDE]
                n = 16 * b + (0 if h < 2 else 4 * (h - 1))
                if i in (0, LEVELS) and not (isinstance(n, int) and n == 0):
                    dve.wait_ge(su_done if i else a_done, n)
                dve.wait_ge(dec_exp, 8 * (4 * b + h) + i + 1)
                if i < LEVELS:
                    level_operand(m_lv[h % 2][:, i, :], dec[:, i % 2, :], k, q, 2 ** i, BLOCK).then_inc(lv_ready, 1)
                    return
                v.tensor_tensor(kd[:, h % 2, :], k, dec[:, i % 2, :], ALU.mult).then_inc(kd_ready, 1)
                dve.wait_ge(eg_ready, 4 * b + h + 1)
                v.scalar_tensor_tensor(out=qe[:, h % 2, :], in0=q, scalar=Q_SCALE, in1=qe[:, h % 2, :], op0=ALU.mult,
                                       op1=ALU.mult).then_inc(qe_ready, 1)

            def operands(b, h):
                dve.wait_ge(q_taken, 4 * b + 4)
                exponent(b, h, 0)
                for i in range(1 + LEVELS):
                    if i < LEVELS:
                        exponent(b, h, i + 1)
                    operand(b, h, i)

            def attention(b):
                def masked(i):
                    n = 16 * b + i
                    dve.wait_ge(a_done, n + 1)
                    if not (isinstance(n, int) and n == 0):
                        dve.wait_ge(at_ready, n)
                    v.tensor_tensor(a_all, ps[:, 2 * (i % 2):2 * (i % 2) + 2, :].rearrange("p a b -> p (a b)"), masks,
                                    ALU.mult).then_inc(a_masked, 1)
                    dve.wait_ge(a_masked, n + 1)
                    if not (isinstance(n, int) and n < 2):
                        dve.wait_ge(o_done, n - 1)
                    v.tensor_reduce(a_t[:, i % 2, :], a_all.rearrange("p (l t) -> p t l", t=P),
                                    mybir.AxisListType.X, ALU.add).then_inc(at_ready, 1)

                masked(0)
                for i in range(HEADS * TILES):
                    h, w, n = i // TILES, i % TILES, 16 * b + i
                    if i + 1 < HEADS * TILES:
                        masked(i + 1)
                    dve.wait_ge(su_done, n + 1)
                    if not (isinstance(n, int) and n == 0):
                        dve.wait_ge(s_ready, n)
                    v.scalar_tensor_tensor(out=state[:, h, :], in0=state[:, h, :], scalar=g_end[:, h, w:w + 1],
                                           in1=ps[:, 6, 0:P], op0=ALU.mult, op1=ALU.add).then_inc(s_ready, 1)
                    gt = gate[:, w, win(h)]
                    dve.wait_ge(o_squared, n + 1)
                    v.tensor_tensor(gt, gt, ps[:, (4, 7)[i % 2], 0:P], ALU.mult).then_inc(o_gated, 1)
                    if i in AHEAD:
                        head, steps = AHEAD[i]
                        if steps[0] == 0:
                            exponent(b, head, 0)
                            exponent(b, head, 1)
                        for step in steps:
                            operand(b, head, step)
                            if step + 2 <= LEVELS:
                                exponent(b, head, step + 2)

            def mixer_output(b, hd):
                dve.wait_ge(o_squared, 16 * b + 16)
                dve.wait_ge(o_gated, 16 * b + 16)
                if hd:
                    dve.wait_ge(ho_squared, HEADS)
                root(ovar[:, :], orstd[:, :], ortmp[:, :], 1.0 / P, ovar_ready, b + 1, oguess_ready, b + 1,
                     osumsq[:, :, :].rearrange("p t h -> p (t h)"))
                for t in (list(range(TILES)) if not hd else [TILES] + list(range(TILES))):
                    rows = slice(0, P) if t < TILES else slice(0, HEAD)
                    for h in range(HEADS):
                        gt = gate[rows, t, h * P:(h + 1) * P]
                        last = v.scalar_tensor_tensor(out=gt, in0=gt, scalar=orstd[rows, 4 * t + h:4 * t + h + 1],
                                                      in1=gn[rows, :], op0=ALU.mult, op1=ALU.mult)
                    if t < TILES:
                        last.then_inc(y_ready, 1)
                for t in range(TILES):
                    dve.wait_ge(y_hi, 4 * b + t + 1)
                    v.tensor_tensor(h_lo[:, 4:8, main(t)], ps[:, t % 2, :].rearrange("p (k n) -> p k n", k=4),
                                    h_hi[:, 4:8, main(t)].bitcast(F32), ALU.subtract).then_inc(y_taken, 1)
                if hd:
                    dve.wait_ge(hh_hi_ready, 2)
                    v.tensor_tensor(h_lo[:, 4:8, 0:HEAD], ps[:, 2, 0:4 * HEAD].rearrange("p (k n) -> p k n", k=4),
                                    h_hi[:, 4:8, 0:HEAD].bitcast(F32), ALU.subtract).then_inc(hh_ready, 1)

            def residual(b, hd):
                for n in range(2):
                    half_residual(b, hd, n, U_OUT + 4 * n + 4, x1_ready, hx1_ready)

            def half_residual(b, hd, n, unit, ready, hready):
                c = slice(n * 512, (n + 1) * 512)
                if ready is x1_ready and n == 0:
                    for t in range(TILES):
                        dve.wait_ge(x_loaded[t], 16 * (b + 1))
                dve.wait_ge(unit_done, UNITS * b + unit)
                for t in range(TILES):
                    v.tensor_tensor(x_tok[:, t, c], x_tok[:, t, c], ps[:, bank(n, t), :], ALU.add).then_inc(ready, 1)
                    if hd and t == 0:
                        v.tensor_tensor(x_tok[0:HEAD, TILES, c], x_tok[0:HEAD, TILES, c],
                                        ps[0:HEAD, bank(n, TILES), :], ALU.add).then_inc(hready, 1)

            def up(b, hd):
                if hd:
                    own.mark(v.memset(ha_ext[:, :, :], 0.0))
                    dve.wait_ge(conv_in_t, 1)
                    own.mark(v.tensor_copy(conv_in[:, :, :], ps[:, 6, 0:FT * 16].rearrange("p (f n) -> p f n", f=FT)))
                    own.settle()

                def tile(j, r, first):
                    ft = 2 * j + r
                    n = FT * b + ft
                    w0 = vec[:, bass.ds(V_CONV_W + ft, 1)]
                    w1 = vec[:, bass.ds(V_CONV_W + FT + ft, 1)]
                    if hd:
                        hae = ha_ext[:, r, :].rearrange("p (n t) -> p n t", n=SEQS)
                        hcv = hconv[:, r, :].rearrange("p (n t) -> p n t", n=SEQS)
                        v.tensor_copy(hae[:, 1:SEQS, 0:2],
                                      conv_in[:, bass.ds(ft, 1), :].rearrange("p a (n r) -> p (a n) r", r=2)).then_inc(
                                          hist_ready, 1)
                        dve.wait_ge(hist_ready, n + 1)
                        dve.wait_ge(ha_taken, n + 1)
                        own.mark(v.tensor_copy(conv_hist[:, bass.ds(ft, 1), :], hae[:, 0:1, N_META:N_META + 2]))
                        v.tensor_copy(conv_out[:, bass.ds(ft, 1), :].rearrange("p a (n r) -> p (a n) r", r=2),
                                      hae[:, 1:SEQS, DEC_SEQ:DEC_SEQ + 2])
                        own.mark(v.scalar_tensor_tensor(out=hcv, in0=hae[:, :, 1:1 + N_META], scalar=w1, in1=hcv,
                                                        op0=ALU.mult, op1=ALU.add))
                        own.settle()
                        v.scalar_tensor_tensor(out=hcv, in0=hae[:, :, 0:N_META], scalar=w0, in1=hcv,
                                               op0=ALU.mult, op1=ALU.add).then_inc(hconv_ready, 1)
                    ae, cv = a_ext[:, r, :], conv[:, r, :]
                    own.mark(v.tensor_copy(ae[:, 0:2], conv_hist[:, bass.ds(ft, 1), :].rearrange("p a b -> p (a b)")))
                    own.settle()
                    dve.wait_ge(a_taken, n + 1)
                    own.mark(v.scalar_tensor_tensor(out=cv, in0=ae[:, 1:1 + BLOCK], scalar=w1, in1=cv, op0=ALU.mult,
                                                    op1=ALU.add))
                    own.settle()
                    v.scalar_tensor_tensor(out=cv, in0=ae[:, 0:BLOCK], scalar=w0, in1=cv, op0=ALU.mult,
                                           op1=ALU.add).then_inc(conv_ready, 1)
                    v.tensor_copy(conv_hist[:, bass.ds(ft, 1), :].rearrange("p a b -> p (a b)"),
                                  ae[:, BLOCK:BLOCK + 2])
                    dve.wait_ge(unit_done, UNITS * b + U_UP + 4 * j + 2 * r + 2)
                    if hd:
                        dve.wait_ge(hgelu_ready, n + 1)
                        v.tensor_tensor(acts[:, bass.ds(ft, 1), 0:N_META], hcv[:, 0:1, :],
                                        ps[:, 4 + r:5 + r, 64:64 + N_META], ALU.mult)
                        v.tensor_tensor(
                            acts[:, bass.ds(ft, 1), N_META:HEAD].rearrange("p a (n t) -> p (a n) t", t=DEC_SEQ),
                            hcv[:, 1:SEQS, 0:DEC_SEQ],
                            ps[:, 4 + r, 64 + N_META:64 + HEAD].rearrange("p (n t) -> p n t", t=DEC_SEQ),
                            ALU.mult).then_inc(hb_taken, 1)
                    dve.wait_ge(gelu_ready, n + 1)
                    v.tensor_tensor(acts[:, bass.ds(ft, 1), HEAD:WIDE].rearrange("p a b -> p (a b)"), gelu[:, r, :],
                                    ps[:, 2 + r, :], ALU.mult).then_inc(act_ready, 1)

                for r in range(2):
                    tile(0, r, True)
                with own.loop(1, FT // 2, 2 * (4 if hd else 2)) as j:
                    for r in range(2):
                        tile(j, r, False)

            def down(b, hd):
                lo = 0 if hd else HEAD
                first = 8 * b + 8

                def pair(n, i):
                    for kk in range(2):
                        dve.wait_ge(act_hi_ready, 2 * FT * b + FT * n + 2 * i + kk + 1)
                        v.tensor_tensor(act_lo[:, kk, lo:WIDE],
                                        acts[:, bass.ds(2 * i + kk, 1), lo:WIDE].rearrange("p a b -> p (a b)"),
                                        act_hi[:, kk, lo:WIDE].bitcast(F32), ALU.subtract).then_inc(act_lo_ready, 1)

                with dve.Fori(0, FT // 2) as i:
                    pair(0, i)
                dve.wait_ge(squared, 12 * b + 12)
                own.settle()
                v.tensor_scalar(var[:, :], sumsq[:, :], 1.0 / D_MODEL, EPS, ALU.mult, ALU.add).then_inc(var_ready, 1)
                half_residual(b, hd, 0, U_DOWN + 12, x2_ready, hx2_ready)
                pair(1, 0)
                root_step(var[:, :], rstd[:, :], rtmp[:, :], guess_ready, 3 * b + 3)
                pair(1, 1)
                scaled(first, x_next, 0)
                scaled(first, x_next, 1)
                for i in range(2, NEXT_AT + 1):
                    pair(1, i)
                for t in range(TILES):
                    pair(1, NEXT_AT + 1 + t)
                    rows(first, 0, x_next, t, 2)
                with dve.Fori(NEXT_AT + 1 + TILES, FT // 2) as i:
                    pair(1, i)
                half_residual(b, hd, 1, U_DOWN + 24, x2_ready, hx2_ready)

            def final_norm(b, hd):
                dve.wait_ge(squared, 12 * b + 16)
                if hd:
                    dve.wait_ge(hsquared, 3)
                root(var[:, :], rstd[:, :], rtmp[:, :], 1.0 / D_MODEL, var_ready, 3 * b + 4, guess_ready, 3 * b + 4,
                     sumsq[:, :])
                for t in range(TILES):
                    v.scalar_tensor_tensor(out=x_tok[:, t, :], in0=x_tok[:, t, :], scalar=rstd[:, t:t + 1],
                                           in1=fg[:, :], op0=ALU.mult, op1=ALU.mult).then_inc(out_ready, 1)
                if hd:
                    x = x_tok[0:HEAD, TILES, :]
                    v.scalar_tensor_tensor(out=x, in0=x, scalar=rstd[0:HEAD, TILES:TILES + 1], in1=fg[0:HEAD, :],
                                           op0=ALU.mult, op1=ALU.mult).then_inc(hout_ready, 1)

            def body(b, hd):
                forget_gates(b, hd)
                dve.wait_ge(g_ready, 4 * b + HEADS)
                for h in range(1 if hd else 2):
                    operands(b, h)
                dve.wait_ge(lv_ready, LEVELS * (4 * b + (1 if hd else 2)))
                pool_branch(b, hd)
                if hd:
                    head_attention()
                    dve.wait_ge(hs_ready, HEADS)
                    operands(b, 1)
                attention(b)
                mixer_output(b, hd)
                residual(b, hd)
                norm(b, 1, hd)
                up(b, hd)
                down(b, hd)
                final_norm(b, hd)

            own.mark(v.memset(sumsq[:, :], 1.0))
            own.mark(v.memset(osumsq[:, :, :], 1.0))
            dve.wait_ge(setup_t, 1)
            own.mark(v.tensor_copy(vec[:, :], ps[:, 0, 0:V_END]))
            own.settle()
            raw = vec[:, V_LB:V_LB + HEADS]
            own.mark(v.tensor_copy(lb[:, 3, :], raw))
            own.settle()
            v.tensor_tensor(lb[:, 0, :], raw, lb[:, 3, :], ALU.subtract).then_inc(vec_ready, 1)
            dve.wait_ge(lb_exp, 1)
            own.mark(v.reciprocal(lb[:, 1, :], lb[:, 0, :]))
            own.settle()
            own.mark(v.tensor_tensor(lb[:, 3, :], lb[:, 0, :], lb[:, 1, :], ALU.mult))
            own.settle()
            own.mark(v.tensor_tensor(lb[:, 0, :], lb[:, 3, :], lb[:, 3, :], ALU.subtract))
            own.settle()
            own.mark(v.tensor_scalar(lb[:, 1, :], lb[:, 0, :], -1.0, 1.0, ALU.mult, ALU.add))
            own.mark(v.tensor_scalar(lb[:, 2, :], lb[:, 0, :], 0.0, None, ALU.is_le))
            own.settle()
            v.tensor_copy(lb[:, 3, :], lb[:, 0, :]).then_inc(setup_done, 1)
            dve.wait_ge(small_loaded, 48)
            dve.wait_ge(tab_loaded, 16)
            norm(0, 0, 1)
            body(0, 1)
            with own.loop(1, BLOCKS, 94) as b:
                body(b, 0)




def kernel(x_prompt, x_sample, state_pool, state_rec, state_conv, meta_tokens, norm1_g, w_in, w_pool, pool_scale,
           lb_raw, rec_norm_g, w_out, norm2_g, w_a, w_b, conv_w, conv_b, w_down, final_g):
    import concourse.bacc as bacc
    from concourse.bass_utils import run_bass_kernel_spmd as run

    given = {
        "x_prompt": x_prompt[0], "x_sample": np.reshape(x_sample, (SAMPLES, D_MODEL)), "state_pool": state_pool[0],
        "state_rec": state_rec[0], "state_conv": state_conv[0], "meta_tokens": meta_tokens,
        "vectors": np.concatenate([np.reshape(v, (-1, P)) for v in
                                   (conv_w, conv_b, norm1_g, norm2_g, lb_raw, pool_scale)]),
        "w_in": w_in[0], "w_pool": w_pool[0], "rec_norm_g": rec_norm_g, "w_out": w_out[0], "w_a": w_a[0],
        "w_b": w_b[0], "w_down": w_down[0], "final_g": final_g, "tables": shape_tables(),
    }
    outs = {
        "y_prompt": (SEQ, D_MODEL), "y_sample": (SAMPLES, D_MODEL), "pool_prompt": (POOL_BUF, D_POOL),
        "rec_prompt": (HEADS, P, P), "conv_prompt": (2, D_FF), "pool_sample": (DEC_BATCH, POOL_BUF, D_POOL),
        "rec_sample": (DEC_BATCH, HEADS, P, P), "conv_sample": (DEC_BATCH, 2, D_FF),
    }
    nc = bacc.Bacc("TRN2", target_bir_lowering=False, num_devices=1)
    arrays = {f"in_{name}": np.ascontiguousarray(a) for name, a in given.items()}
    aps = [nc.dram_tensor(name, a.shape, F32, kind="ExternalInput").ap() for name, a in arrays.items()]
    aps += [nc.dram_tensor(f"out_{name}", shape, F32, kind="ExternalOutput").ap() for name, shape in outs.items()]
    trunk_step(nc, *aps)
    got = run(nc, [arrays], core_ids=[0]).results[0]
    y, ys, pp, rp, cp, pool_s, rs, cs = (got[f"out_{name}"] for name in outs)
    return (y[None], np.reshape(ys, (DEC_BATCH, DEC_SEQ, D_MODEL)), pp[None, None], rp[None, None], cp[None, None],
            pool_s[None], rs[None], cs[None])
```

```python
from contextlib import ExitStack, contextmanager

import numpy as np

import concourse.bass as bass
from concourse import mybir

F32 = mybir.dt.float32
F32R = mybir.dt.float32r
ALU = mybir.AluOpType
ACT = mybir.ActivationFunctionType

P = 128
D_MODEL = 1024
SEQ = 2048
DEC_BATCH = 8
DEC_SEQ = 4
N_META = 16
D_POOL = 512
POOL_BUF = 15
HEADS = 4
D_FF = 2816
EPS = 1e-6
Q_SCALE = float(P) ** -0.5
WINDOWS = (2, 4, 8, 16)

SAMPLES = DEC_BATCH * DEC_SEQ
HEAD = N_META + SAMPLES
SEQS = 1 + DEC_BATCH
BLOCK = 512
BLOCKS = SEQ // BLOCK
TILES = BLOCK // P
WIDE = HEAD + BLOCK
KD = D_MODEL // P
FT = D_FF // P
UNIT = 1024
UNITS = 96
U_F, U_Q, U_GATE, U_V, U_U, U_OUT, U_UP, U_DOWN = 0, 4, 8, 12, 16, 20, 28, 72
LEVELS = 7
HEAD_LEVELS = 4
EXT = POOL_BUF + N_META
NEXT_AT = 3
U_BEHIND = {g: g + 1 for g in range(HEADS - 1)}
POOLED_BEHIND = {0: 0, 1: 1, 2: 2, 11: 3}
PRODUCT_BEHIND = {10 + g: g for g in range(HEADS)}
LOW_BEHIND = {11 + g: g for g in range(HEADS)}
AHEAD = {TILES * (h - 1) - 2 + n: (h, (2 * n, 2 * n + 1)) for h in (2, 3) for n in range(4)}

C_IDENT = 0
C_MASK = C_IDENT + P
C_RESET = C_MASK + (1 + LEVELS) * P
C_HMASK = C_RESET + WIDE
C_SEQ = C_HMASK + (1 + HEAD_LEVELS) * HEAD
C_COUNT = C_SEQ + SEQS
C_END = C_COUNT + len(WINDOWS) * N_META

V_CONV_W, V_CONV_B, V_N1, V_N2, V_LB, V_SCALE, V_END = 0, 66, 88, 96, 104, 108, 112


def shape_tables():
    t = np.zeros((P, C_END), np.float32)
    t[:, C_IDENT:C_IDENT + P] = np.eye(P)
    s, q = np.arange(P)[:, None], np.arange(P)[None, :]

    def level(h):
        return (s // (2 * h) == q // (2 * h)) & (s % (2 * h) < h) & (q % (2 * h) >= h)

    t[:, C_MASK:C_MASK + P] = np.eye(P) * Q_SCALE
    for n in range(LEVELS):
        t[:, C_MASK + (n + 1) * P:C_MASK + (n + 2) * P] = level(2 ** n) * Q_SCALE
    reset = np.ones(WIDE, np.float32)
    reset[0] = 0
    reset[N_META:HEAD:DEC_SEQ] = 0
    reset[HEAD::P] = 0
    t[:, C_RESET:C_RESET + WIDE] = reset
    t[:HEAD, C_HMASK:C_HMASK + HEAD] = np.eye(HEAD) * Q_SCALE
    for n in range(HEAD_LEVELS):
        m = level(2 ** n)[:HEAD, :HEAD] * Q_SCALE
        if 2 ** n >= DEC_SEQ:
            m[:, N_META:] = 0
        t[:HEAD, C_HMASK + (n + 1) * HEAD:C_HMASK + (n + 2) * HEAD] = m
    t[:N_META, C_SEQ] = 1
    for n in range(DEC_BATCH):
        t[N_META + n * DEC_SEQ:N_META + (n + 1) * DEC_SEQ, C_SEQ + 1 + n] = 1
    for g, w in enumerate(WINDOWS):
        t[:, C_COUNT + g * N_META:C_COUNT + (g + 1) * N_META] = 1.0 / np.minimum(np.arange(N_META) + 1, w)
    return t


class Order:

    def __init__(self, engine, sem):
        self.engine, self.sem, self.base, self.n = engine, sem, 0, 0

    def mark(self, instruction):
        instruction.then_inc(self.sem, 1)
        self.n += 1

    def settle(self):
        self.engine.wait_ge(self.sem, self.base + self.n)

    @contextmanager
    def loop(self, lo, hi, marks):
        base, n = self.base, self.n
        with self.engine.Fori(lo, hi) as i:
            self.base, self.n = base + n + (i - lo) * marks, 0
            yield i
            assert self.n == marks, (self.n, marks)
        self.base, self.n = base, n + (hi - lo) * marks


def trunk_step(nc, x_prompt, x_sample, state_pool, state_rec, state_conv, meta_tokens, vectors, w_in, w_pool,
               rec_norm_g, w_out, w_a, w_b, w_down, final_g, tables,
               y_prompt, y_sample, pool_prompt, rec_prompt, conv_prompt, pool_sample, rec_sample, conv_sample):
    with ExitStack() as ctx:
        def sb(name, shape, dt=F32):
            return ctx.enter_context(nc.sbuf_tensor(name, shape, dt))

        def sem(name):
            return ctx.enter_context(nc.semaphore(name))

        h_hi = sb("h_hi", [P, KD, WIDE], F32R)
        h_lo = sb("h_lo", [P, KD, WIDE], F32R)
        x_tok = sb("x_tok", [P, TILES + 1, D_MODEL])
        with nc.sbuf_tensor("w_raw", [P, 4, UNIT], F32) as w_raw:
            pass
        w_lo = sb("w_lo", [P, 4, UNIT], F32R)
        w_hi = sb("w_hi", [P, 4, UNIT], F32R)
        with nc.sbuf_tensor("pooled", [P, HEADS, WIDE], F32) as pooled:
            pass
        act_hi = sb("act_hi", [P, 2, WIDE], F32R)
        act_lo = sb("act_lo", [P, 2, WIDE], F32R)
        tab = sb("tab", [P, C_END])
        vec = sb("vec", [P, V_END])
        wp = sb("wp", [P, HEADS, P])
        gn = sb("gn", [P, P])
        state = sb("state", [P, HEADS, P])
        conv_hist = sb("conv_hist", [P, FT, 2])
        u_hist = sb("u_hist", [P, HEADS, POOL_BUF])
        sumsq = sb("sumsq", [P, TILES + 1])
        var = sb("var", [P, TILES + 1])
        rstd = sb("rstd", [P, TILES + 1])
        rtmp = sb("rtmp", [P, TILES + 1])
        osumsq = sb("osumsq", [P, TILES + 1, HEADS])
        ovar = sb("ovar", [P, (TILES + 1) * HEADS])
        orstd = sb("orstd", [P, (TILES + 1) * HEADS])
        ortmp = sb("ortmp", [P, (TILES + 1) * HEADS])
        lb = sb("lb", [P, 4, HEADS])
        o_junk = sb("o_junk", [P, P])
        g_end = sb("g_end", [P, HEADS, TILES])
        arena = sb("arena", [P, 24956])
        ps = ctx.enter_context(nc.psum_tensor("ps", [P, 8, 512], F32))

        ident = tab[:, C_IDENT:C_IDENT + P]
        masks = tab[:, C_MASK:C_MASK + (1 + LEVELS) * P]
        reset = tab[:, C_RESET:C_RESET + WIDE]
        hmasks = tab[0:HEAD, C_HMASK:C_HMASK + (1 + HEAD_LEVELS) * HEAD]
        gain = [vec[:, V_N1:V_N1 + KD], vec[:, V_N2:V_N2 + KD]]

        def part(at, *shape):
            n = int(np.prod(shape))
            v = arena[:, at:at + n]
            if len(shape) == 2:
                return v.rearrange("p (a b) -> p a b", a=shape[0])
            if len(shape) == 3:
                return v.rearrange("p (a b c) -> p a b c", a=shape[0], b=shape[1])
            return v

        xn = part(12320, 2, D_MODEL)
        t32 = part(14368, 2, 512)
        junk = part(22752, D_MODEL)
        x_next = part(15392, TILES, D_MODEL)
        fg = part(19488, D_MODEL)
        q_t = part(0, HEADS, WIDE)
        k_t = part(2240, HEADS, WIDE)
        g_t = part(4480, HEADS, WIDE)
        gate = part(6720, TILES + 1, 512)
        v_tok = part(9280, TILES + 1, 512)
        f_u = part(11840, 2, WIDE)
        f_low = part(12960, 2, WIDE)
        f_r = part(14080, WIDE)
        m_lv = [part(11840, LEVELS, BLOCK), part(15424, LEVELS, BLOCK)]
        dec = part(19008, 2, BLOCK)
        u_sum = part(23902, 2, POOL_BUF + BLOCK)
        a_all = part(20062, (1 + LEVELS) * P)
        a_sum = part(21086, 4 * P)
        kd_tok = part(21598, 2, P)
        kd = part(21854, 2, BLOCK)
        qe = part(22878, 2, BLOCK)
        hu_ext = part(15424, SEQS, EXT)
        hu_sum = part(15703, 2, SEQS * EXT)
        pool_rows = part(16261, 512)
        u_rows = part(16773, HEADS * SAMPLES)
        pool_in = part(16901, HEADS * DEC_BATCH * POOL_BUF)
        s0 = part(17392, DEC_BATCH, P)
        h_lv = part(18416, HEAD_LEVELS, HEAD)
        h_dec = part(18608, 2 + HEAD_LEVELS, HEAD)
        ha_t = part(18896, HEAD)
        o_feat = part(18944, HEAD)
        ha_all = part(21086, (1 + HEAD_LEVELS) * HEAD)
        h_kd = part(21326, HEAD)
        h_qe = part(21374, HEAD)
        v_seq = [part(22366, 4, P), part(23390, 4, P), part(21422, 1, P)]
        acts = part(0, FT, WIDE)
        a_ext = part(12320, 2, 2 + BLOCK)
        conv = part(13348, 2, BLOCK)
        gelu = part(14372, 2, BLOCK)
        ha_ext = part(15396, 2, SEQS * (2 + N_META))
        hconv = part(15720, 2, SEQS * N_META)
        conv_rows = part(16008, D_FF)
        conv_in = part(18824, FT, 2 * DEC_BATCH)
        conv_out = part(19176, FT, 2 * DEC_BATCH)
        last_rows = part(0, D_POOL)

        raw_loaded = [sem(f"raw_loaded{s}") for s in range(4)]
        w_slot_free = sem("w_slot_free")
        w_hi_ready, w_ready, unit_done = sem("w_hi_ready"), sem("w_ready"), sem("unit_done")
        tab_loaded, vec_loaded, small_loaded = sem("tab_loaded"), sem("vec_loaded"), sem("small_loaded")
        pool_state_loaded, conv_state_loaded, rec_state_loaded = (
            sem("pool_state_loaded"), sem("conv_state_loaded"), sem("rec_state_loaded"))
        x_loaded = [sem(f"x_loaded{t}") for t in range(TILES)]
        x_next_loaded = [sem(f"x_next_loaded{t}") for t in range(TILES)]
        hx_loaded, fg_loaded = sem("hx_loaded"), sem("fg_loaded")
        dve_order, act_order = sem("dve_order"), sem("act_order")
        setup_t, vec_ready, lb_exp, setup_done = sem("setup_t"), sem("vec_ready"), sem("lb_exp"), sem("setup_done")
        squared, hsquared, var_ready, guess_ready = sem("squared"), sem("hsquared"), sem("var_ready"), sem("guess_ready")
        xn_ready, hxn_ready, xt_done, hxt_done = sem("xn_ready"), sem("hxn_ready"), sem("xt_done"), sem("hxt_done")
        t32_ready, ht32_ready, h_hi_ready, hh_hi_ready = (
            sem("t32_ready"), sem("ht32_ready"), sem("h_hi_ready"), sem("hh_hi_ready"))
        h_ready, hh_ready = sem("h_ready"), sem("hh_ready")
        f_taken, f_exp, f_sig, f_ln, g_ready = sem("f_taken"), sem("f_exp"), sem("f_sig"), sem("f_ln"), sem("g_ready")
        q_taken, u_taken, gate_taken, v_taken = sem("q_taken"), sem("u_taken"), sem("gate_taken"), sem("v_taken")
        pooled_ready, pool_done, pool_hi, pool_taken = (
            sem("pooled_ready"), sem("pool_done"), sem("pool_hi"), sem("pool_taken"))
        pool_in_t, pool_in_taken, u_rows_t, u_rows_ready = (
            sem("pool_in_t"), sem("pool_in_taken"), sem("u_rows_t"), sem("u_rows_ready"))
        dec_ready, dec_exp, kd_ready, eg_ready, qe_ready, lv_ready = (
            sem("dec_ready"), sem("dec_exp"), sem("kd_ready"), sem("eg_ready"), sem("qe_ready"), sem("lv_ready"))
        a_done, a_masked, at_ready, kdt_done, kdt_ready, o_done, su_done, s_ready = (
            sem("a_done"), sem("a_masked"), sem("at_ready"), sem("kdt_done"), sem("kdt_ready"),
            sem("o_done"), sem("su_done"), sem("s_ready"))
        o_squared, o_gated = sem("o_squared"), sem("o_gated")
        hdec_ready, hdec_exp, hops_ready, ha_done, hat_ready = (
            sem("hdec_ready"), sem("hdec_exp"), sem("hops_ready"), sem("ha_done"), sem("hat_ready"))
        hkdt_done, hkdt_ready, hof_done, hof_ready, ho_done, ho_squared, ho_gated = (
            sem("hkdt_done"), sem("hkdt_ready"), sem("hof_done"), sem("hof_ready"), sem("ho_done"),
            sem("ho_squared"), sem("ho_gated"))
        v_seq_ready, hs_done, hs_ready, rec_stored = (
            sem("v_seq_ready"), sem("hs_done"), sem("hs_ready"), sem("rec_stored"))
        ovar_ready, oguess_ready, y_ready, yt_done, y_hi, y_taken = (
            sem("ovar_ready"), sem("oguess_ready"), sem("y_ready"), sem("yt_done"), sem("y_hi"), sem("y_taken"))
        x1_product, hx1_product, x1_ready, hx1_ready = (
            sem("x1_product"), sem("hx1_product"), sem("x1_ready"), sem("hx1_ready"))
        var2_ready, guess2_ready, hvar_ready, hguess_ready = (
            sem("var2_ready"), sem("guess2_ready"), sem("hvar_ready"), sem("hguess_ready"))
        a_taken, conv_ready, gelu_ready, act_ready = (
            sem("a_taken"), sem("conv_ready"), sem("gelu_ready"), sem("act_ready"))
        hist_ready, ha_taken, hconv_ready, hgelu_ready, hb_taken = (
            sem("hist_ready"), sem("ha_taken"), sem("hconv_ready"), sem("hgelu_ready"), sem("hb_taken"))
        conv_in_t, conv_in_ready, conv_out_t, conv_out_taken = (
            sem("conv_in_t"), sem("conv_in_ready"), sem("conv_out_t"), sem("conv_out_taken"))
        act_hi_ready, act_lo_ready, act0_used = sem("act_hi_ready"), sem("act_lo_ready"), sem("act0_used")
        x2_ready, hx2_ready, out_ready, hout_ready = (
            sem("x2_ready"), sem("hx2_ready"), sem("out_ready"), sem("hout_ready"))
        y_stored = [sem(f"y_stored{t}") for t in range(TILES)]
        stored, last_t, last_taken = sem("stored"), sem("last_t"), sem("last_taken")

        block = ctx.enter_context(nc.Block())

        def u_ext(hd):
            return part(20062, POOL_BUF + BLOCK) if hd else x_tok[:, TILES, 0:POOL_BUF + BLOCK]

        def win(w):
            return slice(w * P, (w + 1) * P)

        def main(t):
            return slice(HEAD + P * t, HEAD + P * (t + 1))

        def fq_bank(head, hd):
            return head % 2 if hd else head

        def bank(half, tile):
            return (half * (TILES + 1) + tile) % 8

        def exponents(engine, out, g, half, size):
            o = out[:, 0:size].rearrange("p (n t) -> p n t", t=2 * half)
            gg = g[:, 0:size].rearrange("p (n t) -> p n t", t=2 * half)
            bb = gg[:, :, half - 1:half].broadcast_to([P, size // (2 * half), half])
            engine.tensor_tensor(o[:, :, 0:half], bb, gg[:, :, 0:half], ALU.subtract)
            return engine.tensor_tensor(o[:, :, half:2 * half], gg[:, :, half:2 * half], bb, ALU.subtract)

        def exponent(engine, b, h, i):
            g = g_t[:, h, HEAD:WIDE]
            if i == 1:
                if not (isinstance(b, int) and h == 0):
                    engine.wait_ge(kd_ready, 4 * b + h)
            elif not (isinstance(b, int) and h == 0 and i == 0):
                engine.wait_ge(lv_ready, LEVELS * (4 * b + h) + max(i - 1, 0))
            if i == LEVELS:
                gw = g.rearrange("p (w t) -> p w t", t=P)
                engine.tensor_tensor(dec[:, i % 2, :].rearrange("p (w t) -> p w t", t=P),
                                gw[:, :, P - 1:P].broadcast_to([P, TILES, P]), gw, ALU.subtract).then_inc(dec_ready, 1)
            else:
                exponents(engine, dec[:, i % 2, :], g, 2 ** i, BLOCK).then_inc(dec_ready, 1)

        @block.sync
        def _(sp):
            def unit(b, slot, u, dst, src):
                if not (isinstance(b, int) and isinstance(u, int) and b == 0 and u < 4):
                    sp.wait_ge(unit_done, b * UNITS + u - 3)
                sp.dma_start(dst, src).then_inc(raw_loaded[slot], 16)

            def raw(slot, k):
                return w_raw[:, slot, :].rearrange("p (k n) -> p k n", k=k)

            w_in_t = w_in.rearrange("(k p) n -> p k n", p=P)
            wout = w_out.rearrange("(k p) n -> p k n", p=P)
            wa = w_a.rearrange("(k p) n -> p k n", p=P)
            wb = w_b.rearrange("(k p) n -> p k n", p=P)
            wdown = w_down.rearrange("(k p) n -> p k n", p=P)

            def body(b):
                for s in range(4):
                    unit(b, s, U_F + s, raw(s, KD), w_in_t[:, :, 1024 + s * P:1024 + (s + 1) * P])
                for s in range(4):
                    unit(b, s, U_Q + s, raw(s, KD), w_in_t[:, :, 512 + s * P:512 + (s + 1) * P])
                if not isinstance(b, int):
                    store_y(b - 1)
                for s in range(4):
                    unit(b, s, U_GATE + s, raw(s, 2), w_in_t[:, 2 * s:2 * s + 2, 2048:2560])
                if not isinstance(b, int):
                    for t in range(TILES):
                        sp.wait_ge(y_stored[t], 16 * b)
                        sp.dma_start(x_tok[:, t, :], x_prompt[bass.ds(b * BLOCK + P * t, P), :]).then_inc(
                            x_loaded[t], 16)
                for s in range(4):
                    unit(b, s, U_V + s, raw(s, 2), w_in_t[:, 2 * s:2 * s + 2, 1536:2048])
                for s in range(4):
                    unit(b, s, U_U + s, raw(s, KD), w_in_t[:, :, s * P:(s + 1) * P])
                for n in range(2):
                    for s in range(4):
                        unit(b, s, U_OUT + 4 * n + s, raw(s, 2), wout[:, 2 * s:2 * s + 2, n * 512:(n + 1) * 512])
                with sp.Fori(0, FT // 2) as j:
                    for s in range(4):
                        src = (wa, wb)[s % 2]
                        unit(b, s, U_UP + 4 * j + s, raw(s, KD), src[:, :, bass.ds((2 * j + s // 2) * P, P)])
                for n in range(2):
                    cols = slice(n * 512, (n + 1) * 512)
                    for j in range(2):
                        for s in range(4):
                            unit(b, s, U_DOWN + 12 * n + 4 * j + s, raw(s, 2),
                                 wdown[:, 8 * j + 2 * s:8 * j + 2 * s + 2, cols])
                        if (n, j) == (0, 0):
                            sp.wait_ge(act_hi_ready, 2 * FT * b + 1)
                            for t in range(TILES):
                                sp.dma_start(x_next[:, t, :],
                                             x_prompt[bass.ds((b + 1) % BLOCKS * BLOCK + P * t, P), :]).then_inc(
                                                 x_next_loaded[t], 16)
                            sp.dma_start(fg, final_g.rearrange("(a d) -> a d", a=1).broadcast_to([P, D_MODEL])
                                         ).then_inc(fg_loaded, 16)
                    for s in range(4):
                        k = (16, 18, 20, 20)[s]
                        unit(b, s, U_DOWN + 12 * n + 8 + s, raw(s, 2), wdown[:, k:k + 2, cols])

            def store_y(b):
                for t in range(TILES):
                    sp.wait_ge(out_ready, 4 * b + t + 1)
                    sp.dma_start(y_prompt[bass.ds(b * BLOCK + P * t, P), :], x_tok[:, t, :]).then_inc(y_stored[t], 16)

            sp.dma_start(tab[:, :], tables).then_inc(tab_loaded, 16)
            sp.dma_start(junk[0:V_END, 0:P], vectors).then_inc(vec_loaded, 16)
            for t in range(TILES):
                sp.dma_start(x_tok[:, t, :], x_prompt[P * t:P * (t + 1), :]).then_inc(x_loaded[t], 16)
            sp.dma_start(x_tok[0:N_META, TILES, :], meta_tokens).then_inc(hx_loaded, 16)
            sp.dma_start(x_tok[N_META:HEAD, TILES, :], x_sample).then_inc(hx_loaded, 16)
            sp.dma_start(pool_rows[0:DEC_BATCH * POOL_BUF, :], state_pool.rearrange("n t c -> (n t) c")).then_inc(
                pool_state_loaded, 16)
            sp.dma_start(wp[:, :, :], w_pool.rearrange("g c d -> c g d")).then_inc(small_loaded, 16)
            sp.dma_start(gn[:, :], rec_norm_g.broadcast_to([P, P])).then_inc(small_loaded, 16)
            sp.dma_start(pool_sample[:, 0:POOL_BUF - DEC_SEQ, :], state_pool[:, DEC_SEQ:POOL_BUF, :]).then_inc(stored, 16)
            body(0)
            with sp.Fori(1, BLOCKS) as b:
                body(b)
            store_y(BLOCKS - 1)
            for h in range(HEADS):
                sp.wait_ge(s_ready, BLOCKS * HEADS * TILES)
                sp.dma_start(rec_prompt[h], state[:, h, :]).then_inc(stored, 16)
            sp.wait_ge(last_taken, 1)
            sp.dma_start(pool_prompt, last_rows[0:POOL_BUF, :]).then_inc(stored, 16)
            sp.wait_ge(last_taken, 2)
            sp.dma_start(conv_prompt, conv_rows[0:2, :]).then_inc(stored, 16)
            for t in range(TILES):
                sp.wait_ge(y_stored[t], 16 * BLOCKS)
            sp.wait_ge(stored, 16 * (1 + HEADS + 2))

        @block.gpsimd
        def _(pool):
            def units(j):
                for s in range(4):
                    pool.wait_ge(raw_loaded[s], 16 * (j + 1))
                    pool.sem_inc(w_slot_free, 1)
                    nc.gpsimd.tensor_scalar(w_hi[:, s, :], w_raw[:, s, :], 1.0, 1.0, ALU.mult, ALU.mult).then_inc(
                        w_hi_ready, 1)
                    pool.wait_ge(w_hi_ready, 4 * j + s + 1)
                    nc.gpsimd.tensor_tensor(w_lo[:, s, :], w_raw[:, s, :], w_hi[:, s, :].bitcast(F32),
                                            ALU.subtract).then_inc(w_ready, 1)

            with pool.Fori(0, BLOCKS) as b:
                with pool.Fori(0, U_OUT // 4) as j:
                    units(b * (UNITS // 4) + j)
                for h in (2, 3):
                    for i in range(1 + LEVELS):
                        exponent(pool, b, h, i)
                with pool.Fori(U_OUT // 4, UNITS // 4) as j:
                    units(b * (UNITS // 4) + j)

        @block.tensor
        def _(pe):
            def three(out, lhs, rhs, first, last):
                nc.tensor.matmul(out, lhs[0], rhs[0], start=first, stop=False)
                nc.tensor.matmul(out, lhs[1], rhs[0], start=False, stop=False)
                return nc.tensor.matmul(out, lhs[0], rhs[1], start=False, stop=last)

            def wslot(s, k):
                return [w[:, s, :].rearrange("p (k n) -> p k n", k=k) for w in (w_hi, w_lo)]

            def features(s, out, cols):
                w = wslot(s, KD)
                for k in range(KD):
                    last = three(out, (w[0][:, k, :], w[1][:, k, :]), (h_hi[:, k, cols], h_lo[:, k, cols]),
                                 k == 0, k == KD - 1)
                return last

            MAIN = slice(HEAD, WIDE)

            def row_transposes(n, t, first_bank, bank_free):
                pe.wait_ge(xn_ready, n + t + 1)
                for half in range(2):
                    if t >= bank_free:
                        pe.wait_ge(t32_ready, 2 * (n + t - bank_free) + half + 1)
                    for k in range(4):
                        last = nc.tensor.transpose(
                            ps[:, first_bank + half, k * P:(k + 1) * P],
                            xn[:, t % 2, (4 * half + k) * P:(4 * half + k + 1) * P], ident)
                    last.then_inc(xt_done, 1)

            def head_transposes(w):
                pe.wait_ge(hxn_ready, w + 1)
                for k in range(KD):
                    last = nc.tensor.transpose(ps[:, 4, k * HEAD:(k + 1) * HEAD], xn[0:HEAD, 0, k * P:(k + 1) * P],
                                               ident[0:HEAD, 0:HEAD])
                last.then_inc(hxt_done, 1)

            def feature_tile(b, u, i, bank_main, bank_head, hd):
                pe.wait_ge(w_ready, UNITS * b + u + 1)
                last = features(u % 4, ps[:, bank_main, :], MAIN)
                if hd:
                    last = features(u % 4, ps[:, bank_head, 0:HEAD], slice(0, HEAD))
                last.then_inc(unit_done, 1)

            def token_product(out, cols, k, kk, w):
                return three(out, (h_hi[:, k, cols], h_lo[:, k, cols]), (w[0][:, kk, :], w[1][:, kk, :]),
                             k == 0, k == KD - 1)

            def token_tiles(b, u0, banks, hbank, hd, units=range(4)):
                for i in units:
                    pe.wait_ge(w_ready, UNITS * b + u0 + i + 1)
                    w = wslot((u0 + i) % 4, 2)
                    for kk in range(2):
                        for t in range(TILES + hd):
                            cols = main(t) if t < TILES else slice(0, HEAD)
                            out = ps[:, banks[t], :] if t < TILES else ps[0:HEAD, hbank, :]
                            last = token_product(out, cols, 2 * i + kk, kk, w)
                    last.then_inc(unit_done, 1)

            def out_and_norm(b, hd):
                n = 8 * b + 4
                if hd:
                    pe.wait_ge(x1_ready, 2)
                    for i in range(4):
                        pe.wait_ge(w_ready, U_OUT + 4 + i + 1)
                        for kk in range(2):
                            last = token_product(ps[0:HEAD, bank(1, TILES), :], slice(0, HEAD), 2 * i + kk, kk,
                                                 wslot(i, 2))
                    last.then_inc(hx1_product, 1)
                for i in range(4):
                    pe.wait_ge(w_ready, UNITS * b + U_OUT + 4 + i + 1)
                    for t in range(2):
                        for kk in range(2):
                            last = token_product(ps[:, bank(1, t), :], main(t), 2 * i + kk, kk, wslot(i, 2))
                        if i == 3:
                            last.then_inc(x1_product, 1)
                for t in range(2, TILES):
                    final = t == TILES - 1
                    if final:
                        pe.wait_ge(x1_ready, 8 * b + 1)
                    for i in range(4):
                        for kk in range(2):
                            last = token_product(ps[:, bank(1, t), :], main(t), 2 * i + kk, kk, wslot(i, 2))
                        if final:
                            last.then_inc(unit_done, 1)
                    if not final:
                        last.then_inc(x1_product, 1)
                        pe.wait_ge(x1_ready, 8 * b + 4)
                        row_transposes(n, 0, 2, 1)
                    row_transposes(n, t - 1, 2, 1)
                row_transposes(n, TILES - 1, 2, 1)
                if hd:
                    pe.wait_ge(hx1_ready, 2)
                    head_transposes(1)
                pe.wait_ge(h_ready, 2 * (n + TILES))
                if hd:
                    pe.wait_ge(hh_ready, 3)

            def attention(b, hd):
                def scores(i):
                    h, w, n = i // TILES, i % TILES, 16 * b + i
                    if i == 0:
                        pe.wait_ge(g_ready, 4 * b + HEADS)
                    if w == 0:
                        pe.wait_ge(lv_ready, LEVELS * (4 * b + h + 1))
                    if not (isinstance(n, int) and n < 2):
                        pe.wait_ge(a_masked, n - 1)
                    c = main(w)
                    for l in range(1 + LEVELS):
                        out = ps[:, 2 * (i % 2) + l // 4, win(l % 4)]
                        if l == 0:
                            last = nc.tensor.matmul(out, k_t[:, h, c], q_t[:, h, c], start=True, stop=True)
                        else:
                            m = m_lv[h % 2][:, l - 1, win(w)]
                            last = nc.tensor.matmul(out, m, m, start=True, stop=True)
                    last.then_inc(a_done, 1)

                def kd_transposed(i):
                    h, w, n = i // TILES, i % TILES, 16 * b + i
                    if w == 0:
                        pe.wait_ge(kd_ready, 4 * b + h + 1)
                        pe.wait_ge(qe_ready, 4 * b + h + 1)
                    if not (isinstance(n, int) and n < 1):
                        pe.wait_ge(kdt_ready, n)
                    if not (isinstance(n, int) and n < 2):
                        pe.wait_ge(s_ready, n - 1)
                    nc.tensor.transpose(ps[:, 5, 0:P], kd[:, h % 2, win(w)], ident).then_inc(kdt_done, 1)

                def outputs(i):
                    h, w, n = i // TILES, i % TILES, 16 * b + i
                    hc = win(h)
                    o = ps[:, 4, 0:P]
                    pe.wait_ge(at_ready, n + 1)
                    if not (isinstance(n, int) and n < 1):
                        pe.wait_ge(o_squared, n)
                        pe.wait_ge(o_gated, n)
                    for l in range((1 + LEVELS) // 2):
                        nc.tensor.matmul(o, a_sum[:, win(l)], v_tok[:, w, hc], start=l == 0, stop=False)
                    if not (isinstance(n, int) and n < 1):
                        pe.wait_ge(s_ready, n)
                    nc.tensor.matmul(o, qe[:, h % 2, win(w)], state[:, h, :], start=False, stop=True).then_inc(o_done, 1)
                    pe.wait_ge(kdt_ready, n + (2 if i + 1 < HEADS * TILES else 1))
                    nc.tensor.matmul(ps[:, 5, P:2 * P], kd_tok[:, i % 2, :], v_tok[:, w, hc], start=True,
                                     stop=True).then_inc(su_done, 1)

                scores(0)
                scores(1)
                kd_transposed(0)
                for i in range(HEADS * TILES):
                    if i + 1 < HEADS * TILES:
                        kd_transposed(i + 1)
                    outputs(i)
                    if i + 2 < HEADS * TILES:
                        scores(i + 2)
                    if not hd and i in U_BEHIND:
                        u_tile(b, U_BEHIND[i])
                    if not hd and i in PRODUCT_BEHIND:
                        pool_product(b, PRODUCT_BEHIND[i])

            def u_tile(b, g):
                if g >= 2:
                    pe.wait_ge(u_taken, 4 * b + g - 1)
                feature_tile(b, U_U + g, g, 6 + g % 2, None, 0)

            def pool_product(b, g):
                pe.wait_ge(pooled_ready, 4 * b + g + 1)
                if g >= 2:
                    pe.wait_ge(pool_taken, 4 * b + g - 1)
                nc.tensor.matmul(ps[:, 6 + g % 2, :], wp[:, g, :], pooled[:, g, HEAD:WIDE], start=True,
                                 stop=True).then_inc(pool_done, 1)

            def head_attention():
                for h in range(HEADS):
                    hc = win(h)
                    pe.wait_ge(hops_ready, h + 1)
                    if h:
                        pe.wait_ge(hat_ready, h)
                        pe.wait_ge(hkdt_ready, h)
                    else:
                        pe.wait_ge(v_taken, 4)
                    for l in range(1 + HEAD_LEVELS):
                        out = ps[0:HEAD, 0, l * HEAD:(l + 1) * HEAD]
                        if l == 0:
                            last = nc.tensor.matmul(out, k_t[:, h, 0:HEAD], q_t[:, h, 0:HEAD], start=True, stop=True)
                        else:
                            last = nc.tensor.matmul(out, h_lv[:, l - 1, :], h_lv[:, l - 1, :], start=True, stop=True)
                    last.then_inc(ha_done, 1)
                    nc.tensor.transpose(ps[0:HEAD, 5, 0:P], h_kd, ident).then_inc(hkdt_done, 1)
                    if h:
                        pe.wait_ge(u_taken, h)
                    feature_tile(0, U_U + h, h, 6, 7, 1)
                    pe.wait_ge(hat_ready, h + 1)
                    pe.wait_ge(rec_state_loaded, 16 * (h + 1))
                    if h:
                        pe.wait_ge(ho_squared, h)
                        pe.wait_ge(ho_gated, h)
                    for n in range(DEC_BATCH):
                        c = N_META + n * DEC_SEQ
                        nc.tensor.matmul(ps[:, 4, c:c + DEC_SEQ], s0[:, n, :], h_qe[:, c:c + DEC_SEQ], start=n == 0,
                                         stop=False, skip_group_check=True)
                    nc.tensor.matmul(ps[:, 4, N_META:HEAD], v_tok[0:HEAD, TILES, hc], ha_t[0:HEAD, N_META:HEAD],
                                     start=False, stop=True, skip_group_check=True)
                    last = nc.tensor.matmul(ps[:, 4, 0:N_META], v_tok[0:HEAD, TILES, hc], ha_t[0:HEAD, 0:N_META],
                                            start=True, stop=True)
                    last.then_inc(hof_done, 1)
                    pe.wait_ge(hkdt_ready, h + 1)
                    pe.wait_ge(v_seq_ready, h + 1)
                    if h:
                        pe.wait_ge(hs_ready, h)
                    for n0 in range(0, SEQS, 4):
                        m = min(4, SEQS - n0)
                        last = nc.tensor.matmul(ps[:, 1 + n0 // 4, 0:m * P], kd_tok[0:HEAD, 0, :],
                                                v_seq[n0 // 4][0:HEAD, :, :], start=True, stop=True)
                    last.then_inc(hs_done, 1)
                    pe.wait_ge(hof_ready, h + 1)
                    nc.tensor.transpose(ps[0:HEAD, 4, 0:P], o_feat, ident).then_inc(ho_done, 1)

            def body(b, hd):
                if not hd:
                    pe.wait_ge(h_ready, 2 * (8 * b + TILES))
                    pe.wait_ge(x2_ready, 8 * b)
                for i in range(8):
                    if hd:
                        if i in (2, 3, 4, 5):
                            pe.wait_ge(f_taken, i - 1)
                        if i in (6, 7):
                            pe.wait_ge(q_taken, i - 5)
                    elif i >= 4:
                        pe.wait_ge(f_taken, 4 * b + i - 3)
                    feature_tile(b, i, i, fq_bank(i % 4, hd), 2 + i % 2, hd)
                if hd:
                    pe.wait_ge(q_taken, 3)
                token_tiles(b, U_GATE, (4, 5, 6, 7), 2, hd)
                pe.wait_ge(q_taken, 4 * b + 4)
                if hd:
                    pe.wait_ge(gate_taken, 4 * b + 1)
                token_tiles(b, U_V, (0, 1, 2, 3), 4, hd)
                pe.wait_ge(gate_taken, 4 * b + 4)
                if hd:
                    pe.wait_ge(pool_state_loaded, 16)
                    for g in range(HEADS):
                        last = nc.tensor.transpose(ps[:, 6, g * 120:(g + 1) * 120],
                                                   pool_rows[0:120, g * P:(g + 1) * P], ident[0:120, 0:120])
                    last.then_inc(pool_in_t, 1)
                    pe.wait_ge(pool_in_taken, 1)
                    head_attention()
                    pe.wait_ge(hat_ready, HEADS)
                    pe.wait_ge(hs_ready, HEADS)
                    for g in range(HEADS):
                        pe.wait_ge(pooled_ready, g + 1)
                        if g >= 1:
                            pe.wait_ge(pool_taken, g)
                        nc.tensor.matmul(ps[:, g % 2, :], wp[:, g, :], pooled[:, g, HEAD:WIDE], start=True, stop=True)
                        nc.tensor.matmul(ps[:, 2, 0:HEAD], wp[:, g, :], pooled[:, g, 0:HEAD], start=True,
                                         stop=True).then_inc(pool_done, 1)
                    pe.wait_ge(pool_taken, 4)
                else:
                    u_tile(b, 0)
                    pe.wait_ge(v_taken, 4 * b + 4)
                if hd:
                    pe.wait_ge(u_taken, 4)
                    for g in range(HEADS):
                        last = nc.tensor.transpose(ps[0:SAMPLES, 3, g * P:(g + 1) * P],
                                                   u_rows[:, g * SAMPLES:(g + 1) * SAMPLES], ident)
                    last.then_inc(u_rows_t, 1)
                    pe.wait_ge(ho_squared, HEADS)
                    pe.wait_ge(ho_gated, HEADS)
                    pe.wait_ge(u_rows_ready, 1)
                attention(b, hd)
                pe.wait_ge(a_masked, 16 * b + 16)
                pe.wait_ge(pool_taken, 4 * b + 4)
                if hd:
                    pe.wait_ge(o_gated, 16)
                    pe.wait_ge(o_squared, 16)
                banks = [bank(0, t) for t in range(TILES)]
                token_tiles(b, U_OUT, banks, bank(0, TILES), hd, range(2))
                for t in range(TILES):
                    pe.wait_ge(y_ready, 4 * b + t + 1)
                    if t >= 2:
                        pe.wait_ge(y_taken, 4 * b + t - 1)
                    for h in range(HEADS):
                        last = nc.tensor.transpose(ps[:, 6 + t % 2, h * P:(h + 1) * P], gate[:, t, h * P:(h + 1) * P], ident)
                    last.then_inc(yt_done, 1)
                if hd:
                    pe.wait_ge(s_ready, 16)
                    for h in range(HEADS):
                        last = nc.tensor.transpose(ps[:, 5, h * HEAD:(h + 1) * HEAD],
                                                   gate[0:HEAD, TILES, h * P:(h + 1) * P], ident[0:HEAD, 0:HEAD])
                    last.then_inc(hxt_done, 1)
                    pe.wait_ge(hh_ready, 2)
                pe.wait_ge(y_taken, 4 * b + 4)
                token_tiles(b, U_OUT, banks, bank(0, TILES), hd, range(2, 4))
                pe.wait_ge(s_ready, 16 * b + 16)
                out_and_norm(b, hd)
                up(b, hd)
                down(b, hd)

            def up(b, hd):
                if hd:
                    pe.wait_ge(conv_state_loaded, 16)
                    for f in range(FT):
                        last = nc.tensor.transpose(ps[:, 6, f * 16:(f + 1) * 16], conv_rows[0:16, f * P:(f + 1) * P],
                                                   ident[0:16, 0:16])
                    last.then_inc(conv_in_t, 1)

                def pair(j, first):
                    for r in range(2):
                        n = FT * b + 2 * j + r
                        u = UNITS * b + U_UP + 4 * j + 2 * r
                        pe.wait_ge(w_ready, u + 1)
                        if not first:
                            pe.wait_ge(a_taken, n - 1)
                            if hd:
                                pe.wait_ge(hb_taken, n - 1)
                        last = features(2 * r, ps[:, r, :], MAIN)
                        if hd:
                            last = features(2 * r, ps[:, 4 + r, 0:HEAD], slice(0, HEAD))
                        last.then_inc(unit_done, 1)
                        pe.wait_ge(w_ready, u + 2)
                        if not first:
                            pe.wait_ge(act_ready, n - 1)
                        last = features(2 * r + 1, ps[:, 2 + r, :], MAIN)
                        if hd:
                            pe.wait_ge(ha_taken, n + 1)
                            last = features(2 * r + 1, ps[:, 4 + r, 64:64 + HEAD], slice(0, HEAD))
                        last.then_inc(unit_done, 1)

                pair(0, True)
                with pe.Fori(1, FT // 2) as j:
                    pair(j, False)
                if hd:
                    pe.wait_ge(hb_taken, FT)
                    for half in range(2):
                        if half:
                            pe.wait_ge(conv_out_taken, 1)
                        for f in range(11 * half, 11 * half + 11):
                            last = nc.tensor.transpose(ps[0:16, 5 + (f % 11) // 4, (f % 11 % 4) * P:(f % 11 % 4 + 1) * P],
                                                       conv_out[:, f, :], ident)
                        last.then_inc(conv_out_t, 1)
                    pe.wait_ge(conv_out_taken, 2)

            def down(b, hd):
                for n in range(2):
                    def ktile(i, kk, slot, wk, first, fin):
                        d = 2 * FT * b + FT * n + 2 * i + kk
                        pe.wait_ge(act_lo_ready, d + 1)
                        for t in range(TILES + hd):
                            cols = main(t) if t < TILES else slice(0, HEAD)
                            out = ps[:, bank(n, t), :] if t < TILES else ps[0:HEAD, bank(n, t), :]
                            last = three(out, (act_hi[:, kk, cols], act_lo[:, kk, cols]),
                                         [w[:, slot, wk * 512:(wk + 1) * 512] for w in (w_hi, w_lo)], first, fin)
                        return last

                    def pair(i, slot, first):
                        pe.wait_ge(w_ready, UNITS * b + U_DOWN + 12 * n + i + 1)
                        ktile(i, 0, slot, 0, first, False).then_inc(act0_used, 1)
                        ktile(i, 1, slot, 1, False, False).then_inc(unit_done, 1)

                    if n:
                        pe.wait_ge(x2_ready, 8 * b + (2 if hd else 1))
                    pair(0, 0, True)
                    if n:
                        for i in range(1, NEXT_AT):
                            pair(i, i % 4, False)
                        for t in range(TILES):
                            pair(NEXT_AT + t, (NEXT_AT + t) % 4, False)
                            if t == 0:
                                pe.wait_ge(x2_ready, 8 * b + 4)
                            row_transposes(8 * b + 8, t, 2, 1)
                    with pe.Fori(NEXT_AT + TILES if n else 1, 10) as i:
                        pair(i, i % 4, False)
                    for kk in range(2):
                        pe.wait_ge(w_ready, UNITS * b + U_DOWN + 12 * n + 10 + kk + 1)
                        ktile(10, kk, 2 + kk, kk, False, kk == 1).then_inc(unit_done, 1)

            pe.wait_ge(tab_loaded, 16)
            pe.wait_ge(vec_loaded, 16)
            nc.tensor.transpose(ps[:, 0, 0:V_END], junk[0:V_END, 0:P], ident[0:V_END, 0:V_END]).then_inc(setup_t, 1)
            pe.wait_ge(setup_done, 1)
            pe.wait_ge(small_loaded, 32)
            for t in range(TILES):
                row_transposes(0, t, 2 * (t % 2), 2)
            head_transposes(0)
            pe.wait_ge(h_ready, 2 * TILES)
            pe.wait_ge(hh_ready, 1)
            body(0, 1)
            with pe.Fori(1, BLOCKS) as b:
                body(b, 0)
            pe.wait_ge(x2_ready, 8 * BLOCKS)
            for g in range(HEADS):
                last = nc.tensor.transpose(ps[0:POOL_BUF, 0, g * P:(g + 1) * P], u_hist[:, g, :], ident)
            last.then_inc(last_t, 1)
            for f in range(FT):
                last = nc.tensor.transpose(ps[0:2, 1 + f // 4, (f % 4) * P:(f % 4 + 1) * P], conv_hist[:, f, :], ident)
            last.then_inc(last_t, 1)

        @block.scalar
        def _(act):
            own = Order(act, act_order)

            def square(x, t, n):
                if not (isinstance(n, int) and n == 0):
                    act.wait_ge(squared, n)
                nc.scalar.activation(junk, x[:, t, :], ACT.Square, accum_out=sumsq[:, t:t + 1]).then_inc(squared, 1)

            def head_square(n):
                act.wait_ge(squared, n)
                nc.scalar.activation(junk[0:HEAD, :], x_tok[0:HEAD, TILES, :], ACT.Square,
                                     accum_out=sumsq[0:HEAD, TILES:TILES + 1]).then_inc(hsquared, 1)

            def root_guess(v, out, ready, value, signal):
                act.wait_ge(ready, value)
                own.mark(nc.scalar.activation(out, v, ACT.Ln))
                own.settle()
                nc.scalar.activation(out, out, ACT.Exp, scale=-0.5).then_inc(signal, 1)

            def rows_hi(n, t):
                for half in range(2):
                    act.wait_ge(t32_ready, 2 * (n + t) + half + 1)
                    nc.scalar.copy(h_hi[:, 4 * half:4 * half + 4, main(t)],
                                   t32[:, half, :].rearrange("p (k n) -> p k n", k=4)).then_inc(h_hi_ready, 1)

            def head_hi(w):
                act.wait_ge(ht32_ready, w + 1)
                nc.scalar.copy(h_hi[:, :, 0:HEAD], t32[:, 0, 0:KD * HEAD].rearrange("p (k n) -> p k n", k=KD)
                               ).then_inc(hh_hi_ready, 1)

            def decays(b, h, steps):
                for i in steps:
                    act.wait_ge(dec_ready, 8 * (4 * b + h) + i + 1)
                    nc.scalar.activation(dec[:, i % 2, :], dec[:, i % 2, :], ACT.Exp).then_inc(dec_exp, 1)
                    if i == LEVELS:
                        g = g_t[:, h, HEAD:WIDE]
                        if not (isinstance(b, int) and h == 0):
                            act.wait_ge(s_ready, 16 * b if h < 2 else 16 * b + 4 * (h - 1))
                        nc.scalar.activation(g_end[:, h, :], g.rearrange("p (w t) -> p w t", t=P)[:, :, P - 1],
                                             ACT.Exp)
                        nc.scalar.activation(qe[:, h % 2, :], g, ACT.Exp).then_inc(eg_ready, 1)

            def head_recurrence(take_u):
                for h in range(HEADS):
                    act.wait_ge(hdec_ready, h + 1)
                    nc.scalar.activation(h_dec[:, :, :], h_dec[:, :, :], ACT.Exp).then_inc(hdec_exp, 1)
                    if h:
                        act.wait_ge(rec_stored, 16 * h)
                    act.dma_start(s0, state_rec[:, h].rearrange("n d v -> d n v")).then_inc(rec_state_loaded, 16)
                    act.wait_ge(hkdt_done, h + 1)
                    nc.scalar.copy(kd_tok[0:HEAD, 0, :], ps[0:HEAD, 5, 0:P]).then_inc(hkdt_ready, 1)
                    take_u(h)
                    act.wait_ge(hof_done, h + 1)
                    nc.scalar.copy(o_feat, ps[:, 4, 0:HEAD]).then_inc(hof_ready, 1)
                    act.wait_ge(ho_done, h + 1)
                    if h:
                        act.wait_ge(ho_squared, h)
                    nc.scalar.activation(o_junk[0:HEAD, :], ps[0:HEAD, 4, 0:P], ACT.Square,
                                         accum_out=osumsq[0:HEAD, TILES, h:h + 1]).then_inc(ho_squared, 1)
                    act.wait_ge(hs_ready, h + 1)
                    act.dma_start(rec_sample[:, h].rearrange("n d v -> d n v"), s0).then_inc(rec_stored, 16)

            def body(b, hd):
                lo = 0 if hd else HEAD
                for h in range(HEADS):
                    act.wait_ge(f_taken, 4 * b + h + 1)
                    nc.scalar.activation(f_u[:, h % 2, lo:WIDE], f_u[:, h % 2, lo:WIDE], ACT.Exp, scale=-1.0).then_inc(
                        f_exp, 1)
                    act.wait_ge(f_sig, 4 * b + h + 1)
                    nc.scalar.activation(f_u[:, h % 2, lo:WIDE], f_u[:, h % 2, lo:WIDE], ACT.Ln).then_inc(f_ln, 1)
                for h in range(HEADS):
                    act.wait_ge(unit_done, UNITS * b + U_Q + h + 1)
                    if hd:
                        nc.scalar.activation(q_t[:, h, 0:HEAD], ps[:, 2 + h % 2, 0:HEAD], ACT.Silu)
                    nc.scalar.activation(q_t[:, h, HEAD:WIDE], ps[:, fq_bank(h, hd), :], ACT.Silu).then_inc(q_taken, 1)
                nc.scalar.preload_act_table_set("natural_log_exp_and_others")
                for h in range(1 if hd else 2):
                    decays(b, h, range(1 + LEVELS))
                nc.scalar.preload_act_table(ACT.Silu)
                act.wait_ge(unit_done, UNITS * b + U_GATE + 4)
                if hd:
                    nc.scalar.activation(gate[0:HEAD, TILES, :], ps[0:HEAD, 2, :], ACT.Silu)
                for t in range(TILES):
                    nc.scalar.activation(gate[:, t, :], ps[:, 4 + t, :], ACT.Silu).then_inc(gate_taken, 1)
                nc.scalar.preload_act_table_set("natural_log_exp_and_others")
                act.wait_ge(unit_done, UNITS * b + U_V + 4)
                if hd:
                    nc.scalar.copy(v_tok[0:HEAD, TILES, :], ps[0:HEAD, 4, :])
                for t in range(TILES):
                    nc.scalar.copy(v_tok[:, t, :], ps[:, t, :]).then_inc(v_taken, 1)
                def take_u(g):
                    act.wait_ge(unit_done, UNITS * b + U_U + g + 1)
                    if g:
                        act.wait_ge(pooled_ready, 4 * b + g)
                    if hd:
                        he = hu_ext
                        nc.scalar.copy(he[:, 0, POOL_BUF:EXT], ps[:, 7, 0:N_META])
                        nc.scalar.copy(he[:, 1:SEQS, POOL_BUF:POOL_BUF + DEC_SEQ],
                                       ps[:, 7, N_META:HEAD].rearrange("p (n t) -> p n t", t=DEC_SEQ))
                        nc.scalar.copy(u_rows[:, g * SAMPLES:(g + 1) * SAMPLES], ps[:, 7, N_META:HEAD])
                    nc.scalar.copy(u_ext(hd)[:, POOL_BUF:POOL_BUF + BLOCK],
                                   ps[:, 6 if hd else 6 + g % 2, :]).then_inc(u_taken, 1)

                def pool_high(g):
                    act.wait_ge(pool_done, 4 * b + g + 1)
                    sc = vec[:, V_SCALE + g:V_SCALE + g + 1]
                    if hd:
                        nc.scalar.activation(h_hi[:, g, 0:HEAD], ps[:, 2, 0:HEAD], ACT.Copy, scale=sc)
                    nc.scalar.activation(h_hi[:, g, HEAD:WIDE], ps[:, g % 2 if hd else 6 + g % 2, :], ACT.Copy,
                                         scale=sc).then_inc(pool_hi, 1)

                if hd:
                    act.wait_ge(pool_in_taken, 1)
                else:
                    act.wait_ge(hout_ready, 17)
                if hd:
                    head_recurrence(take_u)
                    for g in range(HEADS):
                        pool_high(g)
                else:
                    take_u(0)
                if hd:
                    act.wait_ge(u_rows_t, 1)
                    act.wait_ge(pool_taken, 4)
                    nc.scalar.copy(pool_rows[0:SAMPLES, :], ps[0:SAMPLES, 3, :]).then_inc(u_rows_ready, 1)
                    act.wait_ge(u_rows_ready, 1)
                    act.dma_start(pool_sample[:, POOL_BUF - DEC_SEQ:POOL_BUF, :], pool_rows[0:SAMPLES, :]).then_inc(
                        u_rows_ready, 16)
                    act.wait_ge(rec_stored, 16 * HEADS)
                    act.wait_ge(ho_squared, HEADS)
                    act.wait_ge(u_rows_ready, 17)
                if hd:
                    decays(b, 1, range(1 + LEVELS))
                def kd_tokens(i):
                    n = 16 * b + i
                    act.wait_ge(kdt_done, n + 1)
                    if not (isinstance(n, int) and n < 2):
                        act.wait_ge(su_done, n - 1)
                    nc.scalar.copy(kd_tok[:, i % 2, :], ps[:, 5, 0:P]).then_inc(kdt_ready, 1)

                kd_tokens(0)
                for i in range(HEADS * TILES):
                    h, w, n = i // TILES, i % TILES, 16 * b + i
                    if i + 1 < HEADS * TILES:
                        kd_tokens(i + 1)
                    act.wait_ge(o_done, n + 1)
                    if not (isinstance(n, int) and n == 0):
                        act.wait_ge(o_squared, n)
                    nc.scalar.activation(o_junk[:, :], ps[:, 4, 0:P], ACT.Square,
                                         accum_out=osumsq[:, w, h:h + 1]).then_inc(o_squared, 1)
                    if not hd and i in U_BEHIND:
                        take_u(U_BEHIND[i])
                    if i in AHEAD:
                        decays(b, *AHEAD[i])
                    if not hd and i in PRODUCT_BEHIND:
                        pool_high(PRODUCT_BEHIND[i])
                root_guess(ovar[:, :], orstd[:, :], ovar_ready, b + 1, oguess_ready)
                for t in range(TILES):
                    act.wait_ge(yt_done, 4 * b + t + 1)
                    nc.scalar.copy(h_hi[:, 4:8, main(t)], ps[:, 6 + t % 2, :].rearrange("p (k n) -> p k n", k=4)).then_inc(
                        y_hi, 1)
                if hd:
                    act.wait_ge(hxt_done, 2)
                    nc.scalar.copy(h_hi[:, 4:8, 0:HEAD], ps[:, 5, 0:4 * HEAD].rearrange("p (k n) -> p k n", k=4)
                                   ).then_inc(hh_hi_ready, 1)
                act.wait_ge(hsquared, 1 if hd else 3)
                for t in range(TILES):
                    act.wait_ge(x1_ready, 8 * b + 4 + t + 1)
                    square(x_tok, t, 12 * b + 4 + t)
                    root_guess(var[:, t:t + 1], rstd[:, t:t + 1], var2_ready, 4 * b + t + 1, guess2_ready)
                    if t:
                        rows_hi(8 * b + 4, t - 1)
                rows_hi(8 * b + 4, TILES - 1)
                if hd:
                    act.wait_ge(hx1_ready, 2)
                    head_square(8)
                    root_guess(var[:, TILES:TILES + 1], rstd[:, TILES:TILES + 1], hvar_ready, 1, hguess_ready)
                    head_hi(1)
                if hd:
                    act.dma_start(conv_rows[0:16, :], state_conv.rearrange("n r f -> (n r) f")).then_inc(
                        conv_state_loaded, 16)
                nc.scalar.preload_act_table(ACT.Gelu)

                def up_tile(j, r, first):
                    n = FT * b + 2 * j + r
                    ft = 2 * j + r
                    bias = vec[:, bass.ds(V_CONV_B + ft, 1)]
                    w2 = vec[:, bass.ds(V_CONV_W + 2 * FT + ft, 1)]
                    act.wait_ge(unit_done, UNITS * b + U_UP + 4 * j + 2 * r + 1)
                    if not first:
                        act.wait_ge(act_ready, n - 1)
                    if hd:
                        hae = ha_ext[:, r, :].rearrange("p (n t) -> p n t", n=SEQS)
                        hcv = hconv[:, r, :].rearrange("p (n t) -> p n t", n=SEQS)
                        if not first:
                            act.wait_ge(hb_taken, n - 1)
                        act.wait_ge(hist_ready, n + 1)
                        nc.scalar.copy(hae[:, 0, 2:2 + N_META], ps[:, 4 + r, 0:N_META])
                        own.mark(nc.scalar.copy(hae[:, 1:SEQS, 2:2 + DEC_SEQ],
                                                ps[:, 4 + r, N_META:HEAD].rearrange("p (n t) -> p n t", t=DEC_SEQ)))
                        own.settle()
                        nc.scalar.activation(hcv, hae[:, :, 2:2 + N_META], ACT.Identity, bias=bias, scale=w2).then_inc(
                            ha_taken, 1)
                    nc.scalar.copy(a_ext[:, r, 2:2 + BLOCK], ps[:, r, :])
                    nc.scalar.activation(conv[:, r, :], ps[:, r, :], ACT.Identity, bias=bias, scale=w2).then_inc(
                        a_taken, 1)
                    if hd:
                        act.wait_ge(hconv_ready, n + 1)
                        nc.scalar.activation(hcv, hcv, ACT.Gelu).then_inc(hgelu_ready, 1)
                    act.wait_ge(conv_ready, n + 1)
                    nc.scalar.activation(gelu[:, r, :], conv[:, r, :], ACT.Gelu).then_inc(gelu_ready, 1)

                for r in range(2):
                    up_tile(0, r, True)
                with own.loop(1, FT // 2, 2 if hd else 0) as j:
                    for r in range(2):
                        up_tile(j, r, False)
                if hd:
                    for half in range(2):
                        act.wait_ge(conv_out_t, half + 1)
                        for i in range(3):
                            m = (4, 4, 3)[i] * P
                            at = (11 * half + 4 * i) * P
                            last = nc.scalar.copy(conv_rows[0:16, at:at + m], ps[0:16, 5 + i, 0:m])
                        last.then_inc(conv_out_taken, 1)
                    act.wait_ge(conv_out_taken, 2)
                    act.dma_start(conv_sample.rearrange("n r f -> (n r) f"), conv_rows[0:16, :]).then_inc(
                        conv_out_taken, 16)
                    act.wait_ge(conv_out_taken, 18)
                def split(n, i, kk, first):
                    u = UNITS * b + U_DOWN + 12 * n
                    if not first:
                        if kk == 0:
                            act.wait_ge(act0_used, 20 * b + 10 * n + i)
                        else:
                            act.wait_ge(unit_done, u + i)
                    elif n:
                        act.wait_ge(unit_done, u - 1 + kk)
                    elif kk == 0:
                        act.wait_ge(act_ready, FT * (b + 1))
                        if hd:
                            act.wait_ge(hb_taken, FT)
                    lo = 0 if hd else HEAD
                    nc.scalar.copy(act_hi[:, kk, lo:WIDE],
                                   acts[:, bass.ds(2 * i + kk, 1), lo:WIDE].rearrange("p a b -> p (a b)")).then_inc(
                                       act_hi_ready, 1)

                def pair(n, i, first=False):
                    for kk in range(2):
                        split(n, i, kk, first)

                pair(0, 0, True)
                with act.Fori(1, 5) as i:
                    pair(0, i)
                for t in range(TILES):
                    pair(0, 5 + t)
                    act.wait_ge(x_next_loaded[t], 16 * (b + 1))
                    square(x_next, t, 12 * b + 8 + t)
                for i in range(9, FT // 2):
                    pair(0, i)
                nc.scalar.preload_act_table_set("natural_log_exp_and_others")
                pair(1, 0, True)
                root_guess(var[:, :], rstd[:, :], var_ready, 2 * b + 2, guess_ready)
                for i in range(1, NEXT_AT + 1):
                    pair(1, i)
                for t in range(TILES):
                    pair(1, NEXT_AT + 1 + t)
                    rows_hi(8 * b + 8, t)
                with act.Fori(NEXT_AT + 1 + TILES, FT // 2) as i:
                    pair(1, i)
                act.wait_ge(hsquared, 2 if hd else 3)
                for t in range(TILES):
                    act.wait_ge(x2_ready, 8 * b + 4 + t + 1)
                    square(x_tok, t, 12 * b + 12 + t)
                if hd:
                    act.wait_ge(hx2_ready, 2)
                    head_square(16)
                root_guess(var[:, :], rstd[:, :], var_ready, 2 * b + 3, guess_ready)
                if hd:
                    act.wait_ge(hout_ready, 1)
                    act.dma_start(y_sample, x_tok[N_META:HEAD, TILES, :]).then_inc(hout_ready, 16)

            act.wait_ge(vec_ready, 1)
            nc.scalar.preload_act_table_set("natural_log_exp_and_others")
            nc.scalar.activation(lb[:, 0, :], lb[:, 0, :], ACT.Exp).then_inc(lb_exp, 1)
            act.wait_ge(setup_done, 1)
            for t in range(TILES):
                act.wait_ge(x_loaded[t], 16)
                square(x_tok, t, t)
            act.wait_ge(hx_loaded, 32)
            head_square(4)
            root_guess(var[:, :], rstd[:, :], var_ready, 1, guess_ready)
            for t in range(TILES):
                rows_hi(0, t)
            head_hi(0)
            body(0, 1)
            with own.loop(1, BLOCKS, 7) as b:
                body(b, 0)
            act.wait_ge(last_t, 1)
            nc.scalar.copy(last_rows[0:POOL_BUF, :], ps[0:POOL_BUF, 0, :]).then_inc(last_taken, 1)
            act.wait_ge(last_t, 2)
            for i in range(6):
                m = min(4, FT - 4 * i) * P
                last = nc.scalar.copy(conv_rows[0:2, 4 * i * P:4 * i * P + m], ps[0:2, 1 + i, 0:m])
            last.then_inc(last_taken, 1)
            act.wait_ge(u_rows_ready, 17)
            act.wait_ge(hout_ready, 17)
            act.wait_ge(rec_stored, 16 * HEADS)

        @block.vector
        def _(dve):
            own = Order(dve, dve_order)
            v = nc.vector

            def root(x, y, t, mean, ready, guess, gvalue, src):
                own.settle()
                v.tensor_scalar(x, src, mean, EPS, ALU.mult, ALU.add).then_inc(ready, 1)
                root_step(x, y, t, guess, gvalue)

            def root_step(x, y, t, guess, gvalue):
                dve.wait_ge(guess, gvalue)
                own.mark(v.tensor_tensor(t, y, y, ALU.mult))
                own.settle()
                own.mark(v.tensor_tensor(t, t, x, ALU.mult))
                own.settle()
                own.mark(v.tensor_scalar(t, t, -0.5, 1.5, ALU.mult, ALU.add))
                own.settle()
                own.mark(v.tensor_tensor(y, y, t, ALU.mult))
                own.settle()

            def scaled(n, x, t):
                if t >= 2:
                    dve.wait_ge(xt_done, 2 * (n + t - 1))
                v.tensor_scalar(xn[:, t % 2, :], x[:, t, :], rstd[:, t:t + 1], None, ALU.mult).then_inc(xn_ready, 1)

            def rows(n, w, x, t, bank0, ahead=True):
                for half in range(2):
                    dve.wait_ge(xt_done, 2 * (n + t) + half + 1)
                    if t:
                        dve.wait_ge(h_ready, 2 * (n + t - 1) + half + 1)
                    v.tensor_tensor(t32[:, half, :].rearrange("p (k n) -> p k n", k=4),
                                    ps[:, bank0 + half, :].rearrange("p (k n) -> p k n", k=4),
                                    gain[w][:, 4 * half:4 * half + 4].unsqueeze(2).broadcast_to([P, 4, P]),
                                    ALU.mult).then_inc(t32_ready, 1)
                if ahead and t + 2 < TILES:
                    scaled(n, x, t + 2)
                for half in range(2):
                    dve.wait_ge(h_hi_ready, 2 * (n + t) + half + 1)
                    v.tensor_tensor(h_lo[:, 4 * half:4 * half + 4, main(t)],
                                    t32[:, half, :].rearrange("p (k n) -> p k n", k=4),
                                    h_hi[:, 4 * half:4 * half + 4, main(t)].bitcast(F32),
                                    ALU.subtract).then_inc(h_ready, 1)

            def head_rows(w):
                n, x = 4 * w, (1, 3)[w]
                v.tensor_scalar(xn[0:HEAD, 0, :], x_tok[0:HEAD, TILES, :], rstd[0:HEAD, TILES:TILES + 1], None,
                                ALU.mult).then_inc(hxn_ready, 1)
                dve.wait_ge(hxt_done, x)
                dve.wait_ge(h_ready, 2 * (n + TILES))
                th = t32[:, 0, 0:KD * HEAD].rearrange("p (k n) -> p k n", k=KD)
                v.tensor_tensor(th, ps[:, 4, 0:KD * HEAD].rearrange("p (k n) -> p k n", k=KD),
                                gain[w].unsqueeze(2).broadcast_to([P, KD, HEAD]), ALU.mult).then_inc(ht32_ready, 1)
                dve.wait_ge(hh_hi_ready, x)
                v.tensor_tensor(h_lo[:, :, 0:HEAD], th, h_hi[:, :, 0:HEAD].bitcast(F32), ALU.subtract).then_inc(
                    hh_ready, 1)

            def first_norm():
                dve.wait_ge(squared, TILES)
                dve.wait_ge(hsquared, 1)
                root(var[:, :], rstd[:, :], rtmp[:, :], 1.0 / D_MODEL, var_ready, guess_ready, 1, sumsq[:, :])
                scaled(0, x_tok, 0)
                scaled(0, x_tok, 1)
                for t in range(TILES):
                    rows(0, 0, x_tok, t, 2 * (t % 2))
                head_rows(0)

            def residual_and_norm(b, hd):
                half_residual(b, hd, 0, U_OUT + 4, x1_ready, hx1_ready)
                n = 8 * b + 4
                c = slice(512, 1024)
                if hd:
                    dve.wait_ge(hx1_product, 1)
                    v.tensor_tensor(x_tok[0:HEAD, TILES, c], x_tok[0:HEAD, TILES, c], ps[0:HEAD, bank(1, TILES), :],
                                    ALU.add).then_inc(hx1_ready, 1)
                for t in range(TILES):
                    if t < TILES - 1:
                        dve.wait_ge(x1_product, 3 * b + t + 1)
                    else:
                        dve.wait_ge(unit_done, UNITS * b + U_OUT + 8)
                    v.tensor_tensor(x_tok[:, t, c], x_tok[:, t, c], ps[:, bank(1, t), :], ALU.add).then_inc(x1_ready, 1)
                    one = slice(t, t + 1)
                    dve.wait_ge(squared, 12 * b + 4 + t + 1)
                    root(var[:, one], rstd[:, one], rtmp[:, one], 1.0 / D_MODEL, var2_ready, guess2_ready, 4 * b + t + 1,
                         sumsq[:, one])
                    scaled(n, x_tok, t)
                    if t:
                        rows(n, 1, x_tok, t - 1, 2, False)
                rows(n, 1, x_tok, TILES - 1, 2, False)
                if hd:
                    one = slice(TILES, TILES + 1)
                    dve.wait_ge(hsquared, 2)
                    root(var[:, one], rstd[:, one], rtmp[:, one], 1.0 / D_MODEL, hvar_ready, hguess_ready, 1,
                         sumsq[:, one])
                    head_rows(1)

            def forget_gates(b, hd):
                lo = 0 if hd else HEAD
                c = slice(lo, WIDE)

                def clamp(h):
                    dve.wait_ge(unit_done, UNITS * b + U_F + h + 1)
                    if hd:
                        z = ps[:, 2 + h % 2, 0:HEAD]
                        v.tensor_scalar(f_u[:, h % 2, 0:HEAD], z, -40.0, None, ALU.max)
                        v.tensor_scalar(f_low[:, h % 2, 0:HEAD], z, 40.0, 0.0, ALU.add, ALU.min)
                    z = ps[:, fq_bank(h, hd), :]
                    v.tensor_scalar(f_u[:, h % 2, HEAD:WIDE], z, -40.0, None, ALU.max)
                    v.tensor_scalar(f_low[:, h % 2, HEAD:WIDE], z, 40.0, 0.0, ALU.add, ALU.min).then_inc(f_taken, 1)

                def gates(h):
                    u = f_u[:, h % 2, c]
                    rest = lb[:, 1, h:h + 1]
                    dve.wait_ge(f_exp, 4 * b + h + 1)
                    own.mark(v.tensor_scalar(f_r[:, c], u, 1.0, None, ALU.add))
                    own.settle()
                    own.mark(v.reciprocal(f_r[:, c], f_r[:, c]))
                    own.settle()
                    own.mark(v.scalar_tensor_tensor(out=k_t[:, h, c], in0=u, scalar=rest, in1=f_r[:, c],
                                                    op0=ALU.mult, op1=ALU.mult))
                    own.settle()
                    v.tensor_scalar(u, f_r[:, c], rest, lb[:, 0, h:h + 1], ALU.mult, ALU.add).then_inc(f_sig, 1)

                def cumulate(h):
                    dve.wait_ge(f_ln, 4 * b + h + 1)
                    low = f_low[:, h % 2, c]
                    own.mark(v.scalar_tensor_tensor(out=low, in0=low, scalar=lb[:, 2, h:h + 1], in1=f_u[:, h % 2, c],
                                                    op0=ALU.mult, op1=ALU.add))
                    own.settle()
                    v.tensor_tensor_scan(g_t[:, h, c], reset[:, c], low, 0.0, ALU.mult, ALU.add).then_inc(g_ready, 1)

                clamp(0)
                for h in range(HEADS):
                    gates(h)
                    if h + 1 < HEADS:
                        if h:
                            dve.wait_ge(g_ready, 4 * b + h)
                        clamp(h + 1)
                    cumulate(h)

            def window_sums(src, bufs, size, g, dims):
                now, shift = src, 1
                for i in range(g + 1):
                    nxt = bufs[i % 2]
                    if i:
                        own.settle()
                    start = 2 * shift - 1
                    own.mark(v.tensor_tensor(dims(nxt, start, size), dims(now, start, size),
                                             dims(now, start - shift, size - shift), ALU.add))
                    now, shift = nxt, 2 * shift
                own.settle()
                return now

            def pool_low(b, hd, g):
                dve.wait_ge(pool_hi, 4 * b + g + 1)
                sc = vec[:, V_SCALE + g:V_SCALE + g + 1]
                if hd:
                    v.scalar_tensor_tensor(out=h_lo[:, g, 0:HEAD], in0=ps[:, 2, 0:HEAD], scalar=sc,
                                           in1=h_hi[:, g, 0:HEAD].bitcast(F32), op0=ALU.mult, op1=ALU.subtract)
                v.scalar_tensor_tensor(out=h_lo[:, g, HEAD:WIDE], in0=ps[:, g % 2 if hd else 6 + g % 2, :], scalar=sc,
                                       in1=h_hi[:, g, HEAD:WIDE].bitcast(F32), op0=ALU.mult,
                                       op1=ALU.subtract).then_inc(pool_taken, 1)


            def pool_group(b, hd, g):
                w = WINDOWS[g]
                if hd:
                    dve.wait_ge(pool_in_taken, 1)
                    if g:
                        own.settle()
                        dve.wait_ge(pooled_ready, g)
                    own.mark(v.tensor_copy(
                        hu_ext[:, 1:SEQS, 0:POOL_BUF],
                        pool_in[:, g * 120:(g + 1) * 120].rearrange("p (n t) -> p n t", t=POOL_BUF)))
                    own.settle()
                dve.wait_ge(u_taken, 4 * b + g + 1)
                if hd:
                    own.mark(v.tensor_copy(u_hist[:, g, :], hu_ext[:, 0, EXT - POOL_BUF:EXT]))
                    own.settle()

                    def hview(t, a, z):
                        t = t if len(t.shape) == 3 else t.rearrange("p (n t) -> p n t", n=SEQS)
                        return t[:, :, a:z]
                    s = window_sums(hu_ext, (hu_sum[:, 0, :], hu_sum[:, 1, :]), EXT, g, hview)
                    s = s.rearrange("p (n t) -> p n t", n=SEQS)
                    own.mark(v.tensor_tensor(s[:, 0, POOL_BUF:EXT], s[:, 0, POOL_BUF:EXT],
                                             tab[:, C_COUNT + g * N_META:C_COUNT + (g + 1) * N_META], ALU.mult))
                    own.settle()
                    v.tensor_tensor(pooled[:, g, 0:N_META], s[:, 0, POOL_BUF:EXT], hu_ext[:, 0, POOL_BUF:EXT],
                                    ALU.subtract)
                    v.scalar_tensor_tensor(
                        out=pooled[:, g, N_META:HEAD].rearrange("p (n t) -> p n t", t=DEC_SEQ),
                        in0=s[:, 1:SEQS, POOL_BUF:POOL_BUF + DEC_SEQ], scalar=1.0 / w,
                        in1=hu_ext[:, 1:SEQS, POOL_BUF:POOL_BUF + DEC_SEQ], op0=ALU.mult, op1=ALU.subtract)
                ue = u_ext(hd)
                own.mark(v.tensor_copy(ue[:, 0:POOL_BUF], u_hist[:, g, :]))
                own.settle()
                own.mark(v.tensor_copy(u_hist[:, g, :], ue[:, BLOCK:BLOCK + POOL_BUF]))
                s = window_sums(ue, (u_sum[:, 0, :], u_sum[:, 1, :]), POOL_BUF + BLOCK, g, lambda t, a, z: t[:, a:z])
                v.scalar_tensor_tensor(out=pooled[:, g, HEAD:WIDE], in0=s[:, POOL_BUF:POOL_BUF + BLOCK],
                                       scalar=1.0 / w, in1=ue[:, POOL_BUF:POOL_BUF + BLOCK], op0=ALU.mult,
                                       op1=ALU.subtract).then_inc(pooled_ready, 1)

            def pool_states():
                dve.wait_ge(pool_in_t, 1)
                dve.wait_ge(g_ready, 4)
                own.mark(v.memset(hu_ext, 0.0))
                own.mark(v.memset(hu_sum[:, :, :], 0.0))
                own.settle()
                v.tensor_copy(pool_in, ps[:, 6, 0:480]).then_inc(pool_in_taken, 1)

            def head_attention():
                dve.wait_ge(v_taken, 4)
                dve.wait_ge(q_taken, 4)
                dve.wait_ge(g_ready, 4)
                own.mark(v.memset(h_lv[:, :, :], 0.0))
                own.mark(v.memset(h_dec[:, :, :], 0.0))
                own.settle()
                for h in range(HEADS):
                    g = g_t[:, h, 0:HEAD]
                    gs = g[:, N_META:HEAD].rearrange("p (n t) -> p n t", t=DEC_SEQ)
                    q, k = q_t[:, h, 0:HEAD], k_t[:, h, 0:HEAD]
                    if h:
                        dve.wait_ge(hs_done, h)
                        dve.wait_ge(hs_ready, h)
                    v.tensor_tensor(h_dec[:, 0, 0:N_META], g[:, N_META - 1:N_META].broadcast_to([P, N_META]),
                                    g[:, 0:N_META], ALU.subtract)
                    v.tensor_tensor(h_dec[:, 0, N_META:HEAD].rearrange("p (n t) -> p n t", t=DEC_SEQ),
                                    gs[:, :, DEC_SEQ - 1:DEC_SEQ].broadcast_to([P, DEC_BATCH, DEC_SEQ]), gs,
                                    ALU.subtract)
                    last = v.tensor_copy(h_dec[:, 1, :], g)
                    for l in range(HEAD_LEVELS):
                        last = exponents(v, h_dec[:, 2 + l, :], g, 2 ** l, HEAD if 2 ** l < DEC_SEQ else N_META)
                    last.then_inc(hdec_ready, 1)
                    dve.wait_ge(hdec_exp, h + 1)
                    v.tensor_tensor(h_kd, k, h_dec[:, 0, :], ALU.mult)
                    v.scalar_tensor_tensor(out=h_qe, in0=q, scalar=Q_SCALE, in1=h_dec[:, 1, :], op0=ALU.mult,
                                           op1=ALU.mult)
                    for l in range(HEAD_LEVELS):
                        last = level_operand(h_lv[:, l, :], h_dec[:, 2 + l, :], k, q, 2 ** l,
                                             HEAD if 2 ** l < DEC_SEQ else N_META)
                    last.then_inc(hops_ready, 1)
                    for n0 in range(0, SEQS, 4):
                        m = min(4, SEQS - n0)
                        last = v.tensor_tensor(
                            v_seq[n0 // 4][0:HEAD, :, :],
                            v_tok[0:HEAD, TILES, win(h)].unsqueeze(1).broadcast_to([HEAD, m, P]),
                            tab[0:HEAD, C_SEQ + n0:C_SEQ + n0 + m].unsqueeze(2).broadcast_to([HEAD, m, P]), ALU.mult)
                    last.then_inc(v_seq_ready, 1)
                    dve.wait_ge(ha_done, h + 1)
                    own.mark(v.tensor_tensor(ha_all[0:HEAD, :], ps[0:HEAD, 0, 0:(1 + HEAD_LEVELS) * HEAD], hmasks,
                                             ALU.mult))
                    own.settle()
                    v.tensor_reduce(ha_t[0:HEAD, :], ha_all[0:HEAD, :].rearrange("p (l t) -> p t l", t=HEAD),
                                    mybir.AxisListType.X, ALU.add).then_inc(hat_ready, 1)
                    pool_group(0, 1, h)
                    dve.wait_ge(ho_squared, h + 1)
                    gt = gate[0:HEAD, TILES, h * P:(h + 1) * P]
                    v.tensor_tensor(gt, gt, ps[0:HEAD, 4, 0:P], ALU.mult).then_inc(ho_gated, 1)
                    dve.wait_ge(hs_done, h + 1)
                    v.tensor_copy(state[:, h, :], ps[:, 1, 0:P])
                    for n in range(DEC_BATCH):
                        c = N_META + n * DEC_SEQ + DEC_SEQ - 1
                        i = n + 1
                        last = v.scalar_tensor_tensor(out=s0[:, n, :], in0=s0[:, n, :], scalar=h_dec[:, 1, c:c + 1],
                                                      in1=ps[:, 1 + i // 4, (i % 4) * P:(i % 4 + 1) * P], op0=ALU.mult,
                                                      op1=ALU.add)
                    last.then_inc(hs_ready, 1)

            def level_operand(out, e, k, q, half, size):
                def halves(t):
                    t = t[:, 0:size].rearrange("p (n t) -> p n t", t=2 * half)
                    return t[:, :, 0:half], t[:, :, half:2 * half]
                (ol, orr), (el, er) = halves(out), halves(e)
                v.tensor_tensor(ol, halves(k)[0], el, ALU.mult)
                return v.tensor_tensor(orr, halves(q)[1], er, ALU.mult)

            def operand(b, h, i):
                q, k = q_t[:, h, HEAD:WIDE], k_t[:, h, HEAD:WIDE]
                n = 16 * b + (0 if h < 2 else 4 * (h - 1))
                if i in (0, LEVELS) and not (isinstance(n, int) and n == 0):
                    dve.wait_ge(su_done if i else a_done, n)
                dve.wait_ge(dec_exp, 8 * (4 * b + h) + i + 1)
                if i < LEVELS:
                    level_operand(m_lv[h % 2][:, i, :], dec[:, i % 2, :], k, q, 2 ** i, BLOCK).then_inc(lv_ready, 1)
                    return
                v.tensor_tensor(kd[:, h % 2, :], k, dec[:, i % 2, :], ALU.mult).then_inc(kd_ready, 1)
                dve.wait_ge(eg_ready, 4 * b + h + 1)
                v.scalar_tensor_tensor(out=qe[:, h % 2, :], in0=q, scalar=Q_SCALE, in1=qe[:, h % 2, :], op0=ALU.mult,
                                       op1=ALU.mult).then_inc(qe_ready, 1)

            def operands(b, h):
                dve.wait_ge(q_taken, 4 * b + 4)
                exponent(dve, b, h, 0)
                for i in range(1 + LEVELS):
                    if i < LEVELS:
                        exponent(dve, b, h, i + 1)
                    operand(b, h, i)

            def attention(b, hd):
                def masked(i):
                    n = 16 * b + i
                    dve.wait_ge(a_done, n + 1)
                    if not (isinstance(n, int) and n == 0):
                        dve.wait_ge(at_ready, n)
                    v.tensor_tensor(a_all, ps[:, 2 * (i % 2):2 * (i % 2) + 2, :].rearrange("p a b -> p (a b)"), masks,
                                    ALU.mult).then_inc(a_masked, 1)
                    dve.wait_ge(a_masked, n + 1)
                    if not (isinstance(n, int) and n == 0):
                        dve.wait_ge(o_done, n)
                    v.tensor_tensor(a_sum, a_all[:, 0:4 * P], a_all[:, 4 * P:8 * P], ALU.add).then_inc(at_ready, 1)

                masked(0)
                for i in range(HEADS * TILES):
                    h, w, n = i // TILES, i % TILES, 16 * b + i
                    if i + 1 < HEADS * TILES:
                        masked(i + 1)
                    dve.wait_ge(su_done, n + 1)
                    if not (isinstance(n, int) and n == 0):
                        dve.wait_ge(s_ready, n)
                    v.scalar_tensor_tensor(out=state[:, h, :], in0=state[:, h, :], scalar=g_end[:, h, w:w + 1],
                                           in1=ps[:, 5, P:2 * P], op0=ALU.mult, op1=ALU.add).then_inc(s_ready, 1)
                    gt = gate[:, w, win(h)]
                    dve.wait_ge(o_squared, n + 1)
                    v.tensor_tensor(gt, gt, ps[:, 4, 0:P], ALU.mult).then_inc(o_gated, 1)
                    if not hd and i in LOW_BEHIND:
                        pool_low(b, hd, LOW_BEHIND[i])
                    if not hd and i in POOLED_BEHIND:
                        pool_group(b, hd, POOLED_BEHIND[i])
                    if i in AHEAD:
                        head, steps = AHEAD[i]
                        for step in steps:
                            operand(b, head, step)

            def mixer_output(b, hd):
                dve.wait_ge(o_squared, 16 * b + 16)
                dve.wait_ge(o_gated, 16 * b + 16)
                if hd:
                    dve.wait_ge(ho_squared, HEADS)
                root(ovar[:, :], orstd[:, :], ortmp[:, :], 1.0 / P, ovar_ready, oguess_ready, b + 1,
                     osumsq[:, :, :].rearrange("p t h -> p (t h)"))
                for t in (list(range(TILES)) if not hd else [TILES] + list(range(TILES))):
                    rows = slice(0, P) if t < TILES else slice(0, HEAD)
                    for h in range(HEADS):
                        gt = gate[rows, t, h * P:(h + 1) * P]
                        last = v.scalar_tensor_tensor(out=gt, in0=gt, scalar=orstd[rows, 4 * t + h:4 * t + h + 1],
                                                      in1=gn[rows, :], op0=ALU.mult, op1=ALU.mult)
                    if t < TILES:
                        last.then_inc(y_ready, 1)
                for t in range(TILES):
                    dve.wait_ge(y_hi, 4 * b + t + 1)
                    v.tensor_tensor(h_lo[:, 4:8, main(t)], ps[:, 6 + t % 2, :].rearrange("p (k n) -> p k n", k=4),
                                    h_hi[:, 4:8, main(t)].bitcast(F32), ALU.subtract).then_inc(y_taken, 1)
                if hd:
                    dve.wait_ge(hh_hi_ready, 2)
                    v.tensor_tensor(h_lo[:, 4:8, 0:HEAD], ps[:, 5, 0:4 * HEAD].rearrange("p (k n) -> p k n", k=4),
                                    h_hi[:, 4:8, 0:HEAD].bitcast(F32), ALU.subtract).then_inc(hh_ready, 1)

            def half_residual(b, hd, n, unit, ready, hready):
                c = slice(n * 512, (n + 1) * 512)
                if ready is x1_ready and n == 0:
                    for t in range(TILES):
                        dve.wait_ge(x_loaded[t], 16 * (b + 1))
                dve.wait_ge(unit_done, UNITS * b + unit)
                for t in range(TILES):
                    v.tensor_tensor(x_tok[:, t, c], x_tok[:, t, c], ps[:, bank(n, t), :], ALU.add).then_inc(ready, 1)
                    if hd and t == 0:
                        v.tensor_tensor(x_tok[0:HEAD, TILES, c], x_tok[0:HEAD, TILES, c],
                                        ps[0:HEAD, bank(n, TILES), :], ALU.add).then_inc(hready, 1)

            def up(b, hd):
                if hd:
                    own.mark(v.memset(ha_ext[:, :, :], 0.0))
                    dve.wait_ge(conv_in_t, 1)
                    own.mark(v.tensor_copy(conv_in[:, :, :], ps[:, 6, 0:FT * 16].rearrange("p (f n) -> p f n", f=FT)))
                    own.settle()

                def tile(j, r, first):
                    ft = 2 * j + r
                    n = FT * b + ft
                    w0 = vec[:, bass.ds(V_CONV_W + ft, 1)]
                    w1 = vec[:, bass.ds(V_CONV_W + FT + ft, 1)]
                    if hd:
                        hae = ha_ext[:, r, :].rearrange("p (n t) -> p n t", n=SEQS)
                        hcv = hconv[:, r, :].rearrange("p (n t) -> p n t", n=SEQS)
                        v.tensor_copy(hae[:, 1:SEQS, 0:2],
                                      conv_in[:, bass.ds(ft, 1), :].rearrange("p a (n r) -> p (a n) r", r=2)).then_inc(
                                          hist_ready, 1)
                        dve.wait_ge(hist_ready, n + 1)
                        dve.wait_ge(ha_taken, n + 1)
                        own.mark(v.tensor_copy(conv_hist[:, bass.ds(ft, 1), :], hae[:, 0:1, N_META:N_META + 2]))
                        v.tensor_copy(conv_out[:, bass.ds(ft, 1), :].rearrange("p a (n r) -> p (a n) r", r=2),
                                      hae[:, 1:SEQS, DEC_SEQ:DEC_SEQ + 2])
                        own.mark(v.scalar_tensor_tensor(out=hcv, in0=hae[:, :, 1:1 + N_META], scalar=w1, in1=hcv,
                                                        op0=ALU.mult, op1=ALU.add))
                        own.settle()
                        v.scalar_tensor_tensor(out=hcv, in0=hae[:, :, 0:N_META], scalar=w0, in1=hcv,
                                               op0=ALU.mult, op1=ALU.add).then_inc(hconv_ready, 1)
                    ae, cv = a_ext[:, r, :], conv[:, r, :]
                    own.mark(v.tensor_copy(ae[:, 0:2], conv_hist[:, bass.ds(ft, 1), :].rearrange("p a b -> p (a b)")))
                    own.settle()
                    dve.wait_ge(a_taken, n + 1)
                    own.mark(v.scalar_tensor_tensor(out=cv, in0=ae[:, 1:1 + BLOCK], scalar=w1, in1=cv, op0=ALU.mult,
                                                    op1=ALU.add))
                    own.settle()
                    v.scalar_tensor_tensor(out=cv, in0=ae[:, 0:BLOCK], scalar=w0, in1=cv, op0=ALU.mult,
                                           op1=ALU.add).then_inc(conv_ready, 1)
                    v.tensor_copy(conv_hist[:, bass.ds(ft, 1), :].rearrange("p a b -> p (a b)"),
                                  ae[:, BLOCK:BLOCK + 2])
                    dve.wait_ge(unit_done, UNITS * b + U_UP + 4 * j + 2 * r + 2)
                    if hd:
                        dve.wait_ge(hgelu_ready, n + 1)
                        v.tensor_tensor(acts[:, bass.ds(ft, 1), 0:N_META], hcv[:, 0:1, :],
                                        ps[:, 4 + r:5 + r, 64:64 + N_META], ALU.mult)
                        v.tensor_tensor(
                            acts[:, bass.ds(ft, 1), N_META:HEAD].rearrange("p a (n t) -> p (a n) t", t=DEC_SEQ),
                            hcv[:, 1:SEQS, 0:DEC_SEQ],
                            ps[:, 4 + r, 64 + N_META:64 + HEAD].rearrange("p (n t) -> p n t", t=DEC_SEQ),
                            ALU.mult).then_inc(hb_taken, 1)
                    dve.wait_ge(gelu_ready, n + 1)
                    v.tensor_tensor(acts[:, bass.ds(ft, 1), HEAD:WIDE].rearrange("p a b -> p (a b)"), gelu[:, r, :],
                                    ps[:, 2 + r, :], ALU.mult).then_inc(act_ready, 1)

                for r in range(2):
                    tile(0, r, True)
                with own.loop(1, FT // 2, 2 * (4 if hd else 2)) as j:
                    for r in range(2):
                        tile(j, r, False)

            def down(b, hd):
                lo = 0 if hd else HEAD
                first = 8 * b + 8

                def pair(n, i):
                    for kk in range(2):
                        dve.wait_ge(act_hi_ready, 2 * FT * b + FT * n + 2 * i + kk + 1)
                        v.tensor_tensor(act_lo[:, kk, lo:WIDE],
                                        acts[:, bass.ds(2 * i + kk, 1), lo:WIDE].rearrange("p a b -> p (a b)"),
                                        act_hi[:, kk, lo:WIDE].bitcast(F32), ALU.subtract).then_inc(act_lo_ready, 1)

                with dve.Fori(0, FT // 2) as i:
                    pair(0, i)
                dve.wait_ge(squared, 12 * b + 12)
                own.settle()
                v.tensor_scalar(var[:, :], sumsq[:, :], 1.0 / D_MODEL, EPS, ALU.mult, ALU.add).then_inc(var_ready, 1)
                half_residual(b, hd, 0, U_DOWN + 12, x2_ready, hx2_ready)
                pair(1, 0)
                root_step(var[:, :], rstd[:, :], rtmp[:, :], guess_ready, 2 * b + 2)
                pair(1, 1)
                scaled(first, x_next, 0)
                scaled(first, x_next, 1)
                for i in range(2, NEXT_AT + 1):
                    pair(1, i)
                for t in range(TILES):
                    pair(1, NEXT_AT + 1 + t)
                    rows(first, 0, x_next, t, 2)
                with dve.Fori(NEXT_AT + 1 + TILES, FT // 2) as i:
                    pair(1, i)
                half_residual(b, hd, 1, U_DOWN + 24, x2_ready, hx2_ready)

            def final_norm(b, hd):
                dve.wait_ge(squared, 12 * b + 16)
                if hd:
                    dve.wait_ge(hsquared, 3)
                root(var[:, :], rstd[:, :], rtmp[:, :], 1.0 / D_MODEL, var_ready, guess_ready, 2 * b + 3,
                     sumsq[:, :])
                dve.wait_ge(fg_loaded, 16 * (b + 1))
                for t in range(TILES):
                    v.scalar_tensor_tensor(out=x_tok[:, t, :], in0=x_tok[:, t, :], scalar=rstd[:, t:t + 1],
                                           in1=fg, op0=ALU.mult, op1=ALU.mult).then_inc(out_ready, 1)
                if hd:
                    x = x_tok[0:HEAD, TILES, :]
                    v.scalar_tensor_tensor(out=x, in0=x, scalar=rstd[0:HEAD, TILES:TILES + 1], in1=fg[0:HEAD, :],
                                           op0=ALU.mult, op1=ALU.mult).then_inc(hout_ready, 1)

            def body(b, hd):
                forget_gates(b, hd)
                dve.wait_ge(g_ready, 4 * b + HEADS)
                for h in range(1 if hd else 2):
                    operands(b, h)
                if hd:
                    pool_states()
                    head_attention()
                    for g in range(HEADS):
                        pool_low(b, hd, g)
                    dve.wait_ge(hs_ready, HEADS)
                    operands(b, 1)
                attention(b, hd)
                mixer_output(b, hd)
                residual_and_norm(b, hd)
                up(b, hd)
                down(b, hd)
                final_norm(b, hd)

            own.mark(v.memset(sumsq[:, :], 1.0))
            own.mark(v.memset(osumsq[:, :, :], 1.0))
            dve.wait_ge(setup_t, 1)
            own.mark(v.tensor_copy(vec[:, :], ps[:, 0, 0:V_END]))
            own.settle()
            raw = vec[:, V_LB:V_LB + HEADS]
            own.mark(v.tensor_copy(lb[:, 3, :], raw))
            own.settle()
            v.tensor_tensor(lb[:, 0, :], raw, lb[:, 3, :], ALU.subtract).then_inc(vec_ready, 1)
            dve.wait_ge(lb_exp, 1)
            own.mark(v.reciprocal(lb[:, 1, :], lb[:, 0, :]))
            own.settle()
            own.mark(v.tensor_tensor(lb[:, 3, :], lb[:, 0, :], lb[:, 1, :], ALU.mult))
            own.settle()
            own.mark(v.tensor_tensor(lb[:, 0, :], lb[:, 3, :], lb[:, 3, :], ALU.subtract))
            own.settle()
            own.mark(v.tensor_scalar(lb[:, 1, :], lb[:, 0, :], -1.0, 1.0, ALU.mult, ALU.add))
            own.mark(v.tensor_scalar(lb[:, 2, :], lb[:, 0, :], 0.0, None, ALU.is_le))
            own.settle()
            v.tensor_copy(lb[:, 3, :], lb[:, 0, :]).then_inc(setup_done, 1)
            dve.wait_ge(small_loaded, 32)
            dve.wait_ge(tab_loaded, 16)
            first_norm()
            body(0, 1)
            with own.loop(1, BLOCKS, 106) as b:
                body(b, 0)




def kernel(x_prompt, x_sample, state_pool, state_rec, state_conv, meta_tokens, norm1_g, w_in, w_pool, pool_scale,
           lb_raw, rec_norm_g, w_out, norm2_g, w_a, w_b, conv_w, conv_b, w_down, final_g):
    import concourse.bacc as bacc
    from concourse.bass_utils import run_bass_kernel_spmd as run

    given = {
        "x_prompt": x_prompt[0], "x_sample": np.reshape(x_sample, (SAMPLES, D_MODEL)), "state_pool": state_pool[0],
        "state_rec": state_rec[0], "state_conv": state_conv[0], "meta_tokens": meta_tokens,
        "vectors": np.concatenate([np.reshape(v, (-1, P)) for v in
                                   (conv_w, conv_b, norm1_g, norm2_g, lb_raw, pool_scale)]),
        "w_in": w_in[0], "w_pool": w_pool[0], "rec_norm_g": rec_norm_g, "w_out": w_out[0], "w_a": w_a[0],
        "w_b": w_b[0], "w_down": w_down[0], "final_g": final_g, "tables": shape_tables(),
    }
    outs = {
        "y_prompt": (SEQ, D_MODEL), "y_sample": (SAMPLES, D_MODEL), "pool_prompt": (POOL_BUF, D_POOL),
        "rec_prompt": (HEADS, P, P), "conv_prompt": (2, D_FF), "pool_sample": (DEC_BATCH, POOL_BUF, D_POOL),
        "rec_sample": (DEC_BATCH, HEADS, P, P), "conv_sample": (DEC_BATCH, 2, D_FF),
    }
    nc = bacc.Bacc("TRN2", target_bir_lowering=False, num_devices=1)
    arrays = {f"in_{name}": np.ascontiguousarray(a) for name, a in given.items()}
    aps = [nc.dram_tensor(name, a.shape, F32, kind="ExternalInput").ap() for name, a in arrays.items()]
    aps += [nc.dram_tensor(f"out_{name}", shape, F32, kind="ExternalOutput").ap() for name, shape in outs.items()]
    trunk_step(nc, *aps)
    got = run(nc, [arrays], core_ids=[0]).results[0]
    y, ys, pp, rp, cp, pool_s, rs, cs = (got[f"out_{name}"] for name in outs)
    return (y[None], np.reshape(ys, (DEC_BATCH, DEC_SEQ, D_MODEL)), pp[None, None], rp[None, None], cp[None, None],
            pool_s[None], rs[None], cs[None])
```
